# Optimizing a Trainium2 kernel written in Bass

```python
import math
import jax, jax.numpy as jnp
from jax import lax
import numpy as np

D_MODEL = 1024
BATCH = 1
SEQ = 512
DEPTH = 2
DEC_BATCH = 8
DEC_SEQ = 1
PAST_LEN = 1024
PAGE_SIZE = 128

N_MIXERS = 2
N_CONV_LAYERS = (DEPTH + 1) // 2
N_ATTN_LAYERS = DEPTH // 2
SC_WIDTH = 3
GROUPS = ((128, 1), (512, 4), (2048, 16))
N_GROUPS = len(GROUPS)
H_SLOT = 8
HEAD_DIM = 64
ATTN_WIDTH = H_SLOT * HEAD_DIM
QKV_WIDTH = N_GROUPS * 3 * ATTN_WIDTH
N_BUCKETS = 32
MAX_DISTANCE = 2048
QB = 128
D_FF = 2816
FFN_CONV_WIDTH = 3
EPS = 1e-6
SCALE = HEAD_DIM ** -0.5
NEG = -1e30

kernel_name = 'hybrid_shortconv_dilated_swa_convffn_step'

def rmsnorm(x, g):
    xf = x.astype(jnp.float32)
    r = lax.rsqrt(jnp.mean(xf * xf, axis=-1, keepdims=True) + EPS)
    return (xf * r).astype(x.dtype) * g

def causal_dwconv(u, hist, w):
    width = w.shape[0]
    t = u.shape[1]
    uh = jnp.concatenate([hist.astype(u.dtype), u], axis=1)
    out = w[0] * uh[:, 0:t]
    for j in range(1, width):
        out = out + w[j] * uh[:, j:j + t]
    return out, uh[:, uh.shape[1] - (width - 1):]

def shortconv_mixer(h, hist, w_in, conv_w, w_out):
    bg, cg, xv = jnp.split(h @ w_in, 3, axis=-1)
    conv, new_hist = causal_dwconv(cg * xv, hist, conv_w)
    return (bg * conv) @ w_out, new_hist

def convffn(h, hist, w_gate, w_up, conv_w, conv_b, w_down):
    gconv, new_hist = causal_dwconv(h @ w_gate, hist, conv_w)
    return (jax.nn.silu(gconv + conv_b) * (h @ w_up)) @ w_down, new_hist

def project_qkv(h, w_qkv, q_norm, k_norm):
    b, t, _ = h.shape
    p = (h @ w_qkv).reshape(b, t, N_GROUPS, 3, H_SLOT, HEAD_DIM)
    q = rmsnorm(p[:, :, :, 0], q_norm)
    k = rmsnorm(p[:, :, :, 1], k_norm)
    v = p[:, :, :, 2]
    return q, k, v

def _t5_bucket(dist):
    exact = N_BUCKETS // 2
    n = np.asarray(dist, dtype=np.float32)
    large = exact + np.log(np.maximum(n, 1.0) / exact) / math.log(MAX_DISTANCE / exact) * (N_BUCKETS - exact)
    large = np.minimum(np.floor(large), N_BUCKETS - 1)
    return np.where(n < exact, n, large).astype(np.int32)

def _group_biases(rel_bias):
    out = []
    for g, (win, dil) in enumerate(GROUPS):
        bucket = _t5_bucket(dil * np.arange(win // dil + 1))
        out.append(jnp.take(rel_bias, bucket, axis=0)[:, g * H_SLOT:(g + 1) * H_SLOT].T)
    return out

def dilated_branch(q, span_k, span_v, idx, valid, bias):
    idx_c = np.maximum(idx, 0).astype(np.int32)
    kg = jnp.take(span_k, idx_c, axis=1)
    vg = jnp.take(span_v, idx_c, axis=1)
    logits = jnp.einsum('bqhd,bqkhd->bqhk', q, kg, preferred_element_type=jnp.float32) * SCALE
    logits = logits + bias.astype(jnp.float32)[None, None]
    logits = jnp.where(valid[None, :, None, :], logits, NEG)
    m = jnp.max(logits, axis=-1, keepdims=True)
    e = jnp.exp(logits - m)
    s = jnp.sum(e, axis=-1, keepdims=True)
    out = jnp.einsum('bqhk,bqkhd->bqhd', (e / s).astype(span_v.dtype), vg)
    lse = (m + jnp.log(s))[..., 0]
    return out, lse

def merge_groups(outs, lses):
    w = jax.nn.softmax(jnp.stack(lses, axis=0), axis=0)
    out = w[0][..., None].astype(outs[0].dtype) * outs[0]
    for g in range(1, len(outs)):
        out = out + w[g][..., None].astype(outs[g].dtype) * outs[g]
    return out

def dilated_attention_prompt(q, k, v, biases):
    b, t = q.shape[0], q.shape[1]
    pads = []
    for g, (win, dil) in enumerate(GROUPS):
        pw = ((0, 0), (win, 0), (0, 0), (0, 0))
        pads.append((jnp.pad(k[:, :, g], pw), jnp.pad(v[:, :, g], pw)))
    qi = np.arange(QB, dtype=np.int32)[:, None]

    def block(t0):
        qb = lax.dynamic_slice_in_dim(q, t0, QB, axis=1)
        outs, lses = [], []
        for g, (win, dil) in enumerate(GROUPS):
            back = dil * np.arange(win // dil + 1, dtype=np.int32)[None, :]
            span_k = lax.dynamic_slice_in_dim(pads[g][0], t0, win + QB, axis=1)
            span_v = lax.dynamic_slice_in_dim(pads[g][1], t0, win + QB, axis=1)
            valid = (t0 + jnp.asarray(qi - back, dtype=jnp.int32)) >= 0
            o, l = dilated_branch(qb[:, :, g], span_k, span_v, qi + win - back, valid, biases[g])
            outs.append(o)
            lses.append(l)
        return merge_groups(outs, lses)

    out = lax.map(block, jnp.arange(t // QB, dtype=jnp.int32) * QB)
    out = jnp.moveaxis(out, 0, 1).reshape(b, t, ATTN_WIDTH)
    new_cache = []
    for g, (win, dil) in enumerate(GROUPS):
        keep = min(win, t)
        new_cache.append(jnp.stack([k[:, t - keep:, g], v[:, t - keep:, g]], axis=2))
    return out, new_cache

def dilated_attention_sample(q, k, v, caches, biases):
    b, s = q.shape[0], q.shape[1]
    qi = np.arange(s, dtype=np.int32)[:, None]
    outs, lses, new_cache = [], [], []
    for g, (win, dil) in enumerate(GROUPS):
        cache = caches[g]
        keep = cache.shape[1]
        back = dil * np.arange(win // dil + 1, dtype=np.int32)[None, :]
        span_k = jnp.concatenate([cache[:, :, 0], k[:, :, g]], axis=1)
        span_v = jnp.concatenate([cache[:, :, 1], v[:, :, g]], axis=1)
        idx = keep + qi - back
        o, l = dilated_branch(q[:, :, g], span_k, span_v, idx, jnp.asarray(idx >= 0), biases[g])
        outs.append(o)
        lses.append(l)
        n = span_k.shape[1]
        new_cache.append(jnp.stack([span_k[:, n - keep:], span_v[:, n - keep:]], axis=2))
    return merge_groups(outs, lses).reshape(b, s, ATTN_WIDTH), new_cache

def setup_inputs(seed: int = 0) -> dict:
    key = jax.random.key(seed)
    ks = jax.random.split(key, 24)

    def nrm(k, shape, scale):
        return scale * jax.random.normal(k, shape, jnp.float32)

    buf = [min(win, PAST_LEN) for win, _ in GROUPS]
    return {
        'x_prompt': nrm(ks[0], (BATCH, SEQ, D_MODEL), 1.0),
        'x_sample': nrm(ks[1], (DEC_BATCH, DEC_SEQ, D_MODEL), 1.0),
        'state_sc_conv': nrm(ks[2], (N_CONV_LAYERS, DEC_BATCH, SC_WIDTH - 1, D_MODEL), 1.0),
        'cache_kv_d1': nrm(ks[3], (N_ATTN_LAYERS, DEC_BATCH, buf[0], 2, H_SLOT, HEAD_DIM), 1.0),
        'cache_kv_d4': nrm(ks[4], (N_ATTN_LAYERS, DEC_BATCH, buf[1], 2, H_SLOT, HEAD_DIM), 1.0),
        'cache_kv_d16': nrm(ks[5], (N_ATTN_LAYERS, DEC_BATCH, buf[2], 2, H_SLOT, HEAD_DIM), 1.0),
        'state_ffn_conv': nrm(ks[6], (DEPTH, DEC_BATCH, FFN_CONV_WIDTH - 1, D_FF), 1.0),
        'norm_mix': 1.0 + nrm(ks[7], (DEPTH, D_MODEL), 0.02),
        'norm_ffn': 1.0 + nrm(ks[8], (DEPTH, D_MODEL), 0.02),
        'sc_w_in': nrm(ks[9], (N_CONV_LAYERS, D_MODEL, 3 * D_MODEL), D_MODEL ** -0.5),
        'sc_conv_w': nrm(ks[10], (N_CONV_LAYERS, SC_WIDTH, D_MODEL), SC_WIDTH ** -0.5),
        'sc_w_out': nrm(ks[11], (N_CONV_LAYERS, D_MODEL, D_MODEL), D_MODEL ** -0.5),
        'attn_w_qkv': nrm(ks[12], (N_ATTN_LAYERS, D_MODEL, QKV_WIDTH), D_MODEL ** -0.5),
        'attn_q_norm': 1.0 + nrm(ks[13], (N_ATTN_LAYERS, HEAD_DIM), 0.02),
        'attn_k_norm': 1.0 + nrm(ks[14], (N_ATTN_LAYERS, HEAD_DIM), 0.02),
        'attn_w_out': nrm(ks[15], (N_ATTN_LAYERS, ATTN_WIDTH, D_MODEL), ATTN_WIDTH ** -0.5),
        'rel_bias': nrm(ks[16], (N_BUCKETS, N_GROUPS * H_SLOT), 0.5),
        'ffn_w_gate': nrm(ks[17], (DEPTH, D_MODEL, D_FF), D_MODEL ** -0.5),
        'ffn_w_up': nrm(ks[18], (DEPTH, D_MODEL, D_FF), D_MODEL ** -0.5),
        'ffn_conv_w': nrm(ks[19], (DEPTH, FFN_CONV_WIDTH, D_FF), FFN_CONV_WIDTH ** -0.5),
        'ffn_conv_b': nrm(ks[20], (DEPTH, D_FF), 0.02),
        'ffn_w_down': nrm(ks[21], (DEPTH, D_FF, D_MODEL), D_FF ** -0.5),
    }

def reference(x_prompt, x_sample, state_sc_conv, cache_kv_d1, cache_kv_d4, cache_kv_d16, state_ffn_conv,
              norm_mix, norm_ffn, sc_w_in, sc_conv_w, sc_w_out, attn_w_qkv, attn_q_norm, attn_k_norm,
              attn_w_out, rel_bias, ffn_w_gate, ffn_w_up, ffn_conv_w, ffn_conv_b, ffn_w_down):
    biases = _group_biases(rel_bias)
    xp, xs = x_prompt, x_sample
    bp = xp.shape[0]
    sample_caches = (cache_kv_d1, cache_kv_d4, cache_kv_d16)
    p_sc, s_sc, p_ffn, s_ffn = [], [], [], []
    p_kv = [[] for _ in range(N_GROUPS)]
    s_kv = [[] for _ in range(N_GROUPS)]
    for i in range(DEPTH):
        j = i // N_MIXERS
        hp = rmsnorm(xp, norm_mix[i])
        hs = rmsnorm(xs, norm_mix[i])
        if i % N_MIXERS == 0:
            zero = jnp.zeros((bp, SC_WIDTH - 1, D_MODEL), xp.dtype)
            mp, hist_p = shortconv_mixer(hp, zero, sc_w_in[j], sc_conv_w[j], sc_w_out[j])
            ms, hist_s = shortconv_mixer(hs, state_sc_conv[j], sc_w_in[j], sc_conv_w[j], sc_w_out[j])
            p_sc.append(hist_p)
            s_sc.append(hist_s)
        else:
            qp, kp, vp = project_qkv(hp, attn_w_qkv[j], attn_q_norm[j], attn_k_norm[j])
            op, cp = dilated_attention_prompt(qp, kp, vp, biases)
            qs, ks_, vs = project_qkv(hs, attn_w_qkv[j], attn_q_norm[j], attn_k_norm[j])
            os_, cs = dilated_attention_sample(qs, ks_, vs, [c[j] for c in sample_caches], biases)
            mp = op @ attn_w_out[j]
            ms = os_ @ attn_w_out[j]
            for g in range(N_GROUPS):
                p_kv[g].append(cp[g])
                s_kv[g].append(cs[g])
        xp = xp + mp
        xs = xs + ms
        hp = rmsnorm(xp, norm_ffn[i])
        hs = rmsnorm(xs, norm_ffn[i])
        zero_f = jnp.zeros((bp, FFN_CONV_WIDTH - 1, D_FF), xp.dtype)
        fp, fh_p = convffn(hp, zero_f, ffn_w_gate[i], ffn_w_up[i], ffn_conv_w[i], ffn_conv_b[i], ffn_w_down[i])
        fs, fh_s = convffn(hs, state_ffn_conv[i], ffn_w_gate[i], ffn_w_up[i], ffn_conv_w[i], ffn_conv_b[i], ffn_w_down[i])
        p_ffn.append(fh_p)
        s_ffn.append(fh_s)
        xp = xp + fp
        xs = xs + fs
    return (xp, xs,
            jnp.stack(p_sc, axis=0), jnp.stack(p_kv[0], axis=0), jnp.stack(p_kv[1], axis=0),
            jnp.stack(p_kv[2], axis=0), jnp.stack(p_ffn, axis=0),
            jnp.stack(s_sc, axis=0), jnp.stack(s_kv[0], axis=0), jnp.stack(s_kv[1], axis=0),
            jnp.stack(s_kv[2], axis=0), jnp.stack(s_ffn, axis=0))


_drawn_inputs = setup_inputs


def setup_inputs(seed=0):
    import zlib

    import numpy as np

    out = dict(_drawn_inputs(seed))
    spreads = {}
    factors = {'attn_q_norm': 8.0, 'attn_k_norm': 4.128, 'ffn_conv_b': 5.049}
    for name, (base, spread) in spreads.items():
        noise = np.random.default_rng([zlib.crc32(name.encode()), seed]).standard_normal(out[name].shape)
        drawn = base * np.exp(spread * noise) if base else spread * noise
        out[name] = __import__('jax').numpy.asarray(drawn.astype(out[name].dtype))
    for name, factor in factors.items():
        out[name] = (out[name] * factor).astype(out[name].dtype)
    return out
```

```python
import math
from contextlib import ExitStack

import numpy as np

import concourse.bass as bass
from concourse import mybir

F32 = mybir.dt.float32
F32R = mybir.dt.float32r
ALU = mybir.AluOpType
ACT = mybir.ActivationFunctionType
AX_X = mybir.AxisListType.X

P = 128
D = 1024
DK = D // P
SEQ = 512
NS = 8
HALF = 260
HP = SEQ // 2
HS = NS // 2
FF = 2816
FK = FF // P
H = 8
DH = 64
AW = H * DH
NP_ = AW // P
NG = 3
GROUPS = ((128, 1), (512, 4), (2048, 16))
PAST = 1024
KEEP = tuple(min(w, PAST) for w, _ in GROUPS)
NBACK = tuple(min(w, PAST) // d for w, d in GROUPS)
SCOL = (0, NBACK[0] + 1, NBACK[0] + NBACK[1] + 2)
NSC = sum(NBACK) + NG
NB = 32
NEG = -1e30
BIG = 3.0e38
EPS = 1e-6
SCALE = DH ** -0.5
NCLS = 4
CW = SEQ + 2 + 3 * NS
CO = CW - 2
T0W = SEQ + NCLS - 1
TBW = T0W + 2 * P
V0 = 1024
VW = V0 + 512

PC_MIX, PC_FFN, PC_SCW = 0, 2 * DK, 4 * DK
PC_L = (7 * DK, 7 * DK + 4 * FK)
NPC = 7 * DK + 8 * FK


def t5_bucket(dist):
    exact = NB // 2
    n = np.asarray(dist, dtype=np.float32)
    large = exact + np.log(np.maximum(n, 1.0) / exact) / math.log(2048 / exact) * (NB - exact)
    large = np.minimum(np.floor(large), NB - 1)
    return np.where(n < exact, n, large).astype(np.int32)


def bias_onehot():
    t = np.zeros((NB + 1, VW), np.float32)
    for g, off, n, top in ((0, 0, V0, SEQ - 1), (1, V0, 256, P - 1), (2, V0 + 256, 256, P - 1)):
        step = (1, 1, NCLS)[g]
        dil = GROUPS[g][1]
        for m in range(n):
            d = top - m
            if d >= 0 and d % step == 0 and d // step <= GROUPS[g][0] // dil:
                t[t5_bucket(dil * (d // step)), off + m] = 1.0
            else:
                t[NB, off + m] = NEG
    return t


def sample_onehot():
    t = np.zeros((NB, NSC), np.float32)
    for g in range(NG):
        for j in range(NBACK[g] + 1):
            t[t5_bucket(GROUPS[g][1] * (NBACK[g] - j)), SCOL[g] + j] = 1.0
    return t


class Stage:

    def __init__(self, chunk0, tile0, loads0, per_body, iters, tiles_per_body):
        self.chunk0, self.tile0, self.loads0 = chunk0, tile0, list(loads0)
        self.per_body, self.iters, self.tiles_per_body = per_body, iters, tiles_per_body
        self.slot_per_body = [len(range(s, per_body, 4)) for s in range(4)]
        self.odd = per_body % 2 == 1

    def chunk(self, it, c):
        return it * self.per_body + (self.chunk0 + c)

    def tile(self, it, t):
        return it * self.tiles_per_body + (self.tile0 + t)

    def loads(self, it, c):
        s = c % 4
        return it * (16 * self.slot_per_body[s]) + 16 * (self.loads0[s] + c // 4 + 1)

    def end(self):
        return (self.chunk0 + self.per_body * self.iters, self.tile0 + self.tiles_per_body * self.iters,
                [a + b * self.iters for a, b in zip(self.loads0, self.slot_per_body)])


class Chain:

    def __init__(self, eng, sem):
        self.eng, self.sem, self.base = eng, sem, 0
        self.it, self.per, self.local = 0, 0, 0

    def begin(self, it=0, per=0):
        self.it, self.per, self.local = it, per, 0

    def after(self, ins):
        ins.then_inc(self.sem, 1)
        self.local += 1
        self.eng.wait_ge(self.sem, self.it * self.per + (self.base + self.local))

    def end(self, iters=1):
        assert iters == 1 or self.local == self.per, (self.local, self.per)
        self.base += self.local * iters


def build(nc, x_prompt, x_sample, state_sc, cache1, cache4, cache16, state_ffn, norm_mix, norm_ffn, sc_w_in,
          sc_conv_w, sc_w_out, w_qkv, q_norm, k_norm, attn_w_out, rel_bias, w_gate, w_up, ffn_conv_w, ffn_conv_b,
          w_down, hot, hot_s, y_prompt, y_sample, p_sc, p_kv1, p_kv4, p_kv16, p_ffn, s_sc, s_kv1, s_kv4, s_kv16,
          s_ffn):
    caches = (cache1, cache4, cache16)
    p_kv = (p_kv1, p_kv4, p_kv16)
    s_kv = (s_kv1, s_kv4, s_kv16)
    bias_vec = nc.dram_tensor("bias_vec", (H, VW), F32, kind="Internal").ap()
    bias_tab = nc.dram_tensor("bias_tab", (H, P, TBW), F32, kind="Internal").ap()

    with ExitStack() as ctx:
        def sb(name, shape, dt=F32):
            return ctx.enter_context(nc.sbuf_tensor(name, shape, dt))

        def sem(name):
            return ctx.enter_context(nc.semaphore(name))

        x = sb("x", [P, DK, 2, HALF])
        hh = sb("hh", [P, DK, 2, HALF], F32R)
        hl = sb("hl", [P, DK, 2, HALF], F32R)
        r = sb("r", [P, 2, HALF])
        ssq = sb("ssq", [P, 2, HALF])
        wraw = sb("wraw", [P, 4, DK, P])
        wh = [sb(f"wh{s}", [P, DK, P], F32R) for s in range(2)]
        wl = [sb(f"wl{s}", [P, DK, P], F32R) for s in range(2)]
        u = sb("u", [P, CW])
        cv = sb("cv", [P, CO])
        sv = sb("sv", [P, CO])
        sq = sv[:, 0:2 * HALF].rearrange("p (h n) -> p h n", h=2)
        y32 = sb("y32", [P, 2, HALF])
        t1 = sb("t1", [P, 2, HALF])
        params = sb("params", [P, NPC])
        hist_sc = sb("hist_sc", [P, 16, DK])
        hist_ffn = sb("hist_ffn", [P, 2, 16, FK])
        newh = sb("newh", [P, 18 * FK])
        newh_tok = sb("newh_tok", [P, 4 * P])
        ident = sb("ident", [P, P])
        rms_ones = sb("rms_ones", [P, P])
        head_ones = sb("head_ones", [P, P])
        gq = sb("gq", [P, 2])
        small = sb("small", [P, 8])
        ACTB = 2 * FK * 2 * HALF
        with ExitStack() as same:
            yh_r = same.enter_context(nc.sbuf_tensor("yh", [P, FK, 2, HALF], F32R))[:]
            yl_r = same.enter_context(nc.sbuf_tensor("yl", [P, FK, 2, HALF], F32R))[:]
        big = sb("big", [P, ACTB])
        yh = yh_r.bitcast(F32)
        NYT = NP_
        pos = [NYT * 2 * HALF]

        def attn(cols):
            o = pos[0]
            if o < FK * 2 * HALF < o + cols:
                o = (FK + NYT) * 2 * HALF
            pos[0] = o + cols
            assert pos[0] <= ACTB, pos[0]
            return big[:, o:o + cols]

        TT = SEQ + NS
        qk_t = attn(6 * TT).rearrange("p (t n) -> p t n", t=6)
        v_t = attn(3 * TT).rearrange("p (t n) -> p t n", t=3)
        qka = attn(6 * TT).rearrange("p (t n) -> p t n", t=6)
        tb = attn(2 * TBW).rearrange("p (j n) -> p j n", j=2)
        pos[0] = (FK + NYT) * 2 * HALF
        inv = attn(6 * TT).rearrange("p (t n) -> p t n", t=6)
        lg = attn(6 * P)
        pr = attn(6 * P)
        kv_tok = attn(NG * 4 * 2 * P).rearrange("p (g t k d) -> p g t k d", g=NG, t=4, k=2)
        o32 = t1
        qs = sb("qs", [P, NG, NP_, NS])
        ks = sb("ks", [P, NG, NP_, NS])
        kv_s = sb("kv_s", [NS, NG, 2, AW])
        rb = sb("rb", [NB + 1, NG * H])

        acc = ctx.enter_context(nc.psum_tensor("acc", [P, 2, 2, 512], F32))
        M = ctx.enter_context(nc.psum_tensor("M", [P, 2, 512], F32))
        N = ctx.enter_context(nc.psum_tensor("N", [P, 2, 512], F32))

        chunk_loaded = [sem(f"chunk_loaded{s}") for s in range(4)]
        hi_done = sem("hi_done")
        split_done = sem("split_done")
        chunk_used = sem("chunk_used")
        acc_free = sem("acc_free")
        dve_chain = sem("dve_chain")
        act_chain = sem("act_chain")
        setup_in = sem("setup_in")
        rows_in = sem("rows_in")
        gains_in = sem("gains_in")
        rb_in = sem("rb_in")
        pool_set = sem("pool_set")
        setup_t = sem("setup_t")
        params_ready = sem("params_ready")
        gain_ready = sem("gain_ready")
        xt_ready = sem("xt_ready")
        x_ready = sem("x_ready")
        h_ready = sem("h_ready")
        sq_ready = sem("sq_ready")
        hl_ready = sem("hl_ready")
        ssq_ready = sem("ssq_ready")
        ms_ready = sem("ms_ready")
        r_ready = sem("r_ready")
        u_ready = sem("u_ready")
        c0_ready = sem("c0_ready")
        rows_kept = sem("rows_kept")
        conv_done = sem("conv_done")
        silu_ready = sem("silu_ready")
        y_ready = sem("y_ready")
        yh_ready = sem("yh_ready")
        yl_ready = sem("yl_ready")
        rows_t = sem("rows_t")
        rows_tok = sem("rows_tok")
        vec_mm = sem("vec_mm")
        vec_sb = sem("vec_sb")
        vec_out = sem("vec_out")
        tab_out = sem("tab_out")
        tb_in = sem("tb_in")
        qk_ready = sem("qk_ready")
        qsq_ready = sem("qsq_ready")
        qms_ready = sem("qms_ready")
        inv_ready = sem("inv_ready")
        norm_ready = sem("norm_ready")
        s_ready = sem("s_ready")
        softmax_steps = sem("softmax_steps")
        neg_ready = sem("neg_ready")
        e_ready = sem("e_ready")
        p_ready = sem("p_ready")
        pt_ready = sem("pt_ready")
        pt_act = sem("pt_act")
        pt_dve = sem("pt_dve")
        o_ready = sem("o_ready")
        o_kept = sem("o_kept")
        kvt_ready = sem("kvt_ready")
        kvt_act = sem("kvt_act")
        kvt_dve = sem("kvt_dve")
        kv_out = sem("kv_out")
        samp = sem("samp")
        samp_kt = sem("samp_kt")
        samp_kts = [sem(f"samp_kts{i}") for i in range(2)]
        samp_rows = sem("samp_rows")
        samp_in = [sem(f"samp_in{i}") for i in range(2)]
        samp_v = sem("samp_v")
        samp_vin = sem("samp_vin")
        samp_l = sem("samp_l")
        samp_m = sem("samp_m")
        samp_e = sem("samp_e")
        samp_p = sem("samp_p")
        samp_pt = sem("samp_pt")
        samp_pts = sem("samp_pts")
        samp_o = sem("samp_o")
        fin_t = sem("fin_t")
        fin_s = sem("fin_s")
        fin_xs = sem("fin_xs")
        out_done = sem("out_done")
        copied = sem("copied")

        stages, at = [], (0, 0, [0] * 4)
        for per_body, iters, tiles in ((12, 2, 12), (4, 2, 4), (4, FK // 2, 4), (12, 2, 4),
                                       (9, NP_, 9), (4, 2, 4), (4, FK // 2, 4), (12, 2, 4)):
            stages.append(Stage(*at, per_body, iters, tiles))
            at = stages[-1].end()
        S_IN, S_OUT, S_GU0, S_DN0, S_QKV, S_WO, S_GU1, S_DN1 = stages
        DN_CUT = ((0, 8), (8, 15), (15, 22))

        def kmajor(w):
            return w.rearrange("(k p) n -> p k n", p=P)

        block = ctx.enter_context(nc.Block())

        @block.sync
        def _(sp):
            def load(st, it, c, w, k0, k1, col):
                g = st.chunk(it, c)
                sp.wait_ge(split_done, g + (4 if c == 0 and (st is S_QKV or st is S_WO) else 1))
                sp.dma_start(wraw[:, c % 4, 0:k1 - k0, :], w[:, k0:k1, bass.ds(col, P)]) \
                    .then_inc(chunk_loaded[c % 4], 16)

            w = kmajor(sc_w_in[0])
            with sp.Fori(0, 2) as it:
                for c in range(12):
                    load(S_IN, it, c, w, 0, DK, it * (4 * P) + (c % 3) * D + (c // 3) * P)
            w = kmajor(sc_w_out[0])
            with sp.Fori(0, 2) as it:
                for c in range(4):
                    load(S_OUT, it, c, w, 0, DK, it * (4 * P) + c * P)

            def ffn(layer, gu, dn):
                wg, wu, wd = kmajor(w_gate[layer]), kmajor(w_up[layer]), kmajor(w_down[layer])
                with sp.Fori(0, FK // 2) as it:
                    for c in range(4):
                        load(gu, it, c, (wg, wu)[c % 2], 0, DK, it * (2 * P) + (c // 2) * P)
                with sp.Fori(0, 2) as it:
                    for c in range(12):
                        load(dn, it, c, wd, *DN_CUT[c % 3], it * (4 * P) + (c // 3) * P)

            ffn(0, S_GU0, S_DN0)
            w = kmajor(w_qkv[0])
            with sp.Fori(0, NP_) as it:
                for c in range(9):
                    load(S_QKV, it, c, w, 0, DK, it * P + c * AW)
            w = kmajor(attn_w_out[0])
            with sp.Fori(0, 2) as it:
                for c in range(4):
                    load(S_WO, it, c, w, 0, NP_, it * (4 * P) + c * P)
            ffn(1, S_GU1, S_DN1)

        @block.gpsimd
        def _(pool):
            pool.memset(ident[:], 0.0).then_inc(pool_set, 1)
            pool.memset(rms_ones[:], 1.0 / D).then_inc(pool_set, 1)
            pool.memset(head_ones[:], 0.0).then_inc(pool_set, 1)
            pool.wait_ge(pool_set, 3)
            pool.affine_select(out=ident[:], in_=ident[:], compare_op=ALU.not_equal, fill=1.0, base=0,
                               pattern=[[-1, P]], channel_multiplier=1).then_inc(pool_set, 1)
            for i in range(2):
                pool.wait_ge(pool_set, 4 + i)
                s = slice(i * DH, i * DH + DH)
                pool.memset(head_ones[s, s], 1.0 / DH).then_inc(pool_set, 1)

            flat_in = [c.rearrange("l b n k h d -> (l b) (n k h d)") for c in caches]
            flat_out = [c.rearrange("l b n k h d -> (l b) (n k h d)") for c in s_kv]
            row = 2 * AW
            plan = [(2, (KEEP[2] - 1) // 3, 3, 352), (1, KEEP[1] - 1, 1, 512), (0, KEEP[0] - 1, 1, 128)]
            with pool.Fori(0, NS) as b:
                n = 0
                for g, rows, pieces, desc in plan:
                    for i in range(pieces):
                        pool.wait_ge(chunk_used, b * 24 + (8 + 5 * n))
                        n += 1
                        lo = i * rows * row
                        pool.dma_start(
                            flat_out[g][bass.ds(b, 1), lo:lo + rows * row].rearrange("o (a c) -> (o a) c", a=desc),
                            flat_in[g][bass.ds(b, 1), lo + row:lo + row + rows * row]
                            .rearrange("o (a c) -> (o a) c", a=desc)).then_inc(copied, 16)
            pool.wait_ge(copied, 16 * NS * 5)

        GAIN = (PC_MIX, PC_FFN, PC_MIX + DK, PC_FFN + DK)

        def ahead(st, c):
            if not st.odd:
                return [((c + 2) // st.per_body, (c + 2) % st.per_body)]
            if c == st.per_body - 2:
                return []
            if c == st.per_body - 1:
                return [(1, 0), (1, 1)]
            return [(0, c + 2)]

        def prompt(a):
            return a[:, :, 0:HP]

        def sample(a):
            return a[:, :, HP:HALF]

        u_prompt = u[:, 2:2 + SEQ].rearrange("p (h n) -> p h n", h=2)
        u_rows = u[:, 2 + SEQ:CW].rearrange("p (b w) -> p b w", w=3)
        u_new = u_rows[:, :, 2].rearrange("p (h n) -> p h n", h=2)

        def conv_rows(a):
            return a[:, SEQ + 2:CO:3].rearrange("p (h n) -> p h n", h=2)

        def conv_prompt(a):
            return a[:, 0:SEQ].rearrange("p (h n) -> p h n", h=2)

        UNITS = [(hh_, c) for hh_ in range(2) for c in range(NCLS)]
        PTS = lg

        pos[0] = NYT * 2 * HALF
        qblk = attn(NG * NP_ * NS * 64).rearrange("p (g q b m) -> p g q b m", g=NG, q=NP_, b=NS)
        kvb = attn(2 * NG * AW).rearrange("p (s g n) -> p s g n", s=2, g=NG)
        pos[0] = (FK + NYT) * 2 * HALF
        kts = attn(2 * NP_ * NSC).rearrange("p (s q n) -> p s q n", s=2, q=NP_)
        pts = attn(4 * 64).rearrange("p (g m) -> p g m", g=4)
        vnew = attn(NS * AW).rearrange("p (b n) -> p b n", b=NS)
        sl = attn(NSC + 1)
        se = attn(NSC + 1)
        snew = attn(4)
        hots = attn(NSC + 1)
        rbs = attn(NG * 64).rearrange("p (g b h) -> p g b h", g=NG, b=NS)
        os_ = attn(NP_ * NS).rearrange("p (q b) -> p q b", q=NP_)

        xin = big[:, 0:4 * D].rearrange("p (t n) -> p t n", t=4)
        xs_in = big[0:NS, 4 * D:5 * D]
        rows = big[:, 5 * D:5 * D + 10 * P].rearrange("p (t n) -> p t n", t=10)
        hotb = big[0:NB + 1, 5 * D + 10 * P:5 * D + 10 * P + VW]
        vec_sb_t = big[0:H, 8 * D:8 * D + VW]
        ytok = big[:, 0:4 * D].rearrange("p (s n) -> p s n", s=4)
        xs_c = big[:, 4 * D:4 * D + DK * NS].rearrange("p (k n) -> p k n", k=DK)
        ys_tok = big[0:NS, 5 * D:6 * D]

        OUT_ALL = 16 * (2 + 2 * 5 + 5)

        def copy_kt(eng, b, q, act_engine):
            src = acc[:, (b * NP_ + q) % 2, 0, 0:NSC - NG]
            off = 0
            for g in range(NG):
                dst = kts[:, b % 2, q, SCOL[g]:SCOL[g] + NBACK[g]]
                s = src[:, off:off + NBACK[g]]
                new = kts[:, b % 2, q, SCOL[g] + NBACK[g]:SCOL[g] + NBACK[g] + 1]
                off += NBACK[g]
                if act_engine:
                    eng.activation(dst, s, ACT.Copy)
                    last = eng.activation(new, ks[:, g, q, b:b + 1], ACT.Copy)
                else:
                    eng.tensor_copy(dst, s)
                    last = eng.tensor_copy(new, ks[:, g, q, b:b + 1])
            last.then_inc(samp_kts[(b * NP_ + q) % 2], 1)

        YOFF = (0, NP_ + 1)

        @block.scalar
        def _(act):
            ch = Chain(act, act_chain)
            for t in range(4):
                act.dma_start(xin[:, t, :], x_prompt[0, t * P:(t + 1) * P, :]).then_inc(setup_in, 16)
            act.dma_start(xs_in, x_sample.rearrange("b s n -> (b s) n")).then_inc(setup_in, 16)
            act.dma_start(rows[0:2 * DK, 0, :], norm_mix.rearrange("l (k p) -> (l k) p", p=P)).then_inc(rows_in, 16)
            act.dma_start(rows[2 * DK:4 * DK, 0, :], norm_ffn.rearrange("l (k p) -> (l k) p", p=P)) \
                .then_inc(rows_in, 16)
            act.dma_start(rows[4 * DK:7 * DK, 0, :], sc_conv_w.rearrange("l j (k p) -> (l j k) p", p=P)) \
                .then_inc(rows_in, 16)
            for i in range(2):
                act.dma_start(rows[0:3 * FK, 1 + i, :], ffn_conv_w[i].rearrange("j (k p) -> (j k) p", p=P)) \
                    .then_inc(rows_in, 16)
                act.dma_start(rows[3 * FK:4 * FK, 1 + i, :],
                              ffn_conv_b[i:i + 1, :].rearrange("o (k p) -> (o k) p", p=P)).then_inc(rows_in, 16)
            act.dma_start(rows[:, 3, :], state_sc.rearrange("l b w (k p) -> (l b w k) p", p=P)).then_inc(rows_in, 16)
            for i in range(2):
                hr = state_ffn[i].rearrange("b w (k p) -> (b w k) p", p=P)
                for j in range(3):
                    n = min(P, 16 * FK - j * P)
                    act.dma_start(rows[0:n, 4 + 3 * i + j, :], hr[j * P:j * P + n, :]).then_inc(rows_in, 16)
            for i in range(2):
                act.dma_start(gq[i * DH:(i + 1) * DH, 0:1], q_norm.rearrange("o d -> d o")).then_inc(gains_in, 16)
                act.dma_start(gq[i * DH:(i + 1) * DH, 1:2], k_norm.rearrange("o d -> d o")).then_inc(gains_in, 16)
            act.dma_start(rb[0:NB, :], rel_bias).then_inc(rb_in, 16)
            act.dma_start(hotb, hot).then_inc(rb_in, 16)

            def split_hi(st, it, c):
                act.wait_ge(chunk_loaded[c % 4], st.loads(it, c))
                nc.scalar.activation(wh[c % 2][:], wraw[:, c % 4], ACT.Copy).then_inc(hi_done, 1)

            def step(st, it, c, last=False):
                g = st.chunk(it, c)
                act.wait_ge(chunk_used, g + 1)
                if last and c >= st.per_body - 2:
                    return
                for di, cc in ahead(st, c):
                    split_hi(st, it + di, cc)

            def gained(norm, m, n):
                act.wait_ge(x_ready, n + 1)
                c = GAIN[norm]
                act.wait_ge(ssq_ready, n + 1)
                nc.scalar.activation(hh[:, bass.ds(m, 1)], x[:, bass.ds(m, 1)], ACT.Copy,
                                     scale=params[:, bass.ds(m + c, 1)]).then_inc(h_ready, 1)
                nc.scalar.activation(sq, x[:, bass.ds(m, 1)].rearrange("p o h n -> p (o h) n"),
                                     ACT.Square).then_inc(sq_ready, 1)

            def rms(norm):
                act.wait_ge(ms_ready, 2 * norm + 2)
                ch.after(nc.scalar.activation(r[:], r[:], ACT.Ln))
                nc.scalar.activation(r[:], r[:], ACT.Exp, scale=-0.5).then_inc(r_ready, 1)

            def conv_act(v, f, hist, keep, nk, wcol, bcol):
                act.wait_ge(conv_done, v + 1)
                act.wait_ge(rows_kept, v + 1)
                ch.after(nc.scalar.activation(u_rows[:, :, 0:2],
                                              hist[:, :, bass.ds(f, 1)].rearrange("p (b w) o -> p b (w o)", w=2),
                                              ACT.Copy))
                act.wait_ge(u_ready, v + 1)
                if bcol is None:
                    nc.scalar.activation(cv[:], u[:, 0:CO], ACT.Copy,
                                         scale=params[:, bass.ds(f + wcol, 1)]).then_inc(c0_ready, 1)
                else:
                    nc.scalar.activation(cv[:], u[:, 0:CO], ACT.Identity, bias=params[:, bass.ds(f + bcol, 1)],
                                         scale=params[:, bass.ds(f + wcol, 1)]).then_inc(c0_ready, 1)
                k = newh[:, 0:18 * nk].rearrange("p (x f) -> p x f", f=nk)[:, :, bass.ds(f, 1)]
                nc.scalar.activation(k[:, 0:16].rearrange("p (b w) o -> p b (w o)", w=2), u_rows[:, :, 1:3], ACT.Copy)
                nc.scalar.activation(k[:, 16:18].rearrange("p w o -> p (w o)"), u[:, SEQ:SEQ + 2],
                                     ACT.Copy).then_inc(rows_kept, 1)

            def y_hi(n, slot):
                act.wait_ge(y_ready, n + 1)
                nc.scalar.activation(yh_r[:, bass.ds(slot, 1)].rearrange("p o h n -> p (o h) n"), y32[:],
                                     ACT.Copy).then_inc(yh_ready, 1)

            act.wait_ge(params_ready, 1)
            nc.scalar.preload_act_table(ACT.Copy)
            for c in range(2):
                split_hi(S_IN, 0, c)
            for m in range(DK):
                gained(0, m, m)
            act.wait_ge(vec_sb, 1)
            act.dma_start(bias_vec, vec_sb_t).then_inc(vec_out, 16)
            rms(0)
            ch.end()

            nc.scalar.preload_act_table(ACT.Silu)
            with act.Fori(0, 2) as it:
                ch.begin(it, 4)
                for j in range(4):
                    for c in range(3):
                        step(S_IN, it, 3 * j + c)
                    v = it * 4 + j
                    conv_act(v, v, hist_sc, newh, DK, PC_SCW, None)
                    y_hi(v, v)
            ch.end(2)
            act.wait_ge(rows_tok, 1)
            act.dma_start(s_sc.rearrange("l b w (k p) -> (l b w k) p", p=P), newh_tok[:, 0:P]).then_inc(out_done, 16)
            act.dma_start(p_sc.rearrange("l b w (k p) -> (l b w k) p", p=P), newh_tok[0:16, P:2 * P]) \
                .then_inc(out_done, 16)

            def ffn(layer, gu, dn, norm, v0, y0, x0, next_norm):
                nc.scalar.preload_act_table(ACT.Silu)
                pc = PC_L[layer]
                with act.Fori(0, FK // 2) as it:
                    ch.begin(it, 2)
                    for i in range(2):
                        f = it * 2 + i
                        step(gu, it, 2 * i)
                        conv_act(f + v0, f, hist_ffn[:, layer], newh, FK, pc, pc + 3 * FK)
                        act.wait_ge(conv_done, f + (v0 + 2))
                        nc.scalar.activation(sv[:], cv[:], ACT.Silu).then_inc(silu_ready, 1)
                        step(gu, it, 2 * i + 1)
                        y_hi(f + y0, f)
                ch.end(FK // 2)
                rows_out(layer)

                def down(it, last):
                    for c in range(12):
                        step(dn, it, c, last)
                        if c % 3 == 2 and next_norm is not None:
                            m = it * 4 + c // 3
                            gained(next_norm, m, m + x0)
                if next_norm is None:
                    down(0, False)
                    down(1, True)
                else:
                    with act.Fori(0, 2) as it:
                        down(it, False)
                    ch.begin()
                    rms(next_norm)
                    ch.end()

            def rows_out(layer):
                act.wait_ge(rows_tok, layer + 2)
                srows = s_ffn[layer].rearrange("b w (k p) -> (b w k) p", p=P)
                prows = p_ffn[layer].rearrange("b w (k p) -> (b w k) p", p=P)
                ns, nt = 16 * FK, 18 * FK // 4
                for j in range(4):
                    lo, hi = j * nt, (j + 1) * nt
                    if lo < ns:
                        n = min(hi, ns) - lo
                        act.dma_start(srows[lo:lo + n, :], newh_tok[0:n, j * P:(j + 1) * P]).then_inc(out_done, 16)
                    if hi > ns:
                        a = max(lo, ns)
                        act.dma_start(prows[a - ns:hi - ns, :], newh_tok[a - lo:nt, j * P:(j + 1) * P]) \
                            .then_inc(out_done, 16)

            act.wait_ge(vec_out, 16)
            for off, step_, w, dst in ((NCLS * (P - 1), NCLS, T0W, 0), (V0 + P - 1, 1, P, T0W),
                                       (V0 + 256 + P - 1, 1, P, T0W + P)):
                act.dma_start(bias_tab[:, :, dst:dst + w],
                              bass.AP(bias_vec.tensor, off, [[VW, H], [-step_, P], [1, w]])).then_inc(tab_out, 16)
            with act.Fori(0, 2) as it:
                for c in range(4):
                    step(S_OUT, it, c)
                    gained(1, it * 4 + c, it * 4 + (c + DK))
            ch.begin()
            rms(1)
            ch.end()
            ffn(0, S_GU0, S_DN0, 1, DK, DK, 2 * DK, 2)

            act.wait_ge(tab_out, 48)
            nc.scalar.preload_act_table_set("natural_log_exp_and_others")

            def exp_unit(n):
                act.wait_ge(neg_ready, n + 1)
                nc.scalar.activation(pr[:], lg[:], ACT.Exp, bias=small[:, 1:2], scale=-1.0,
                                     accum_out=small[:, 2:3]).then_inc(e_ready, 1)

            def pt_copy(n):
                act.wait_ge(pt_ready, n + 1)
                nc.scalar.activation(PTS[:, 512:768], N[:, 1, 0:256], ACT.Copy).then_inc(pt_act, 1)

            def head_rms(pair, i):
                q = pair * 6 + i
                act.wait_ge(qms_ready, q + 1)
                t = inv[:, i, :].rearrange("p (h n) -> p h n", h=2)
                ch.after(nc.scalar.activation(t, N[:, :, 0:HALF], ACT.Ln, bias=small[:, 7:8]))
                nc.scalar.activation(t, t, ACT.Exp, scale=-0.5).then_inc(inv_ready, 1)

            def project(pair, attend):
                i = 0
                pend = None
                for c in range(9):
                    if attend and c >= 1:
                        pt_copy((pair - 1) * 8 + c - 1)
                    if pend is not None:
                        head_rms(pair, pend)
                        pend = None
                    if attend and c < 8:
                        exp_unit((pair - 1) * 8 + c)
                    step(S_QKV, pair, c)
                    if c % 3 < 2:
                        q = pair * 6 + i
                        act.wait_ge(qk_ready, q + 1)
                        nc.scalar.activation(sq, qk_t[:, i, :].rearrange("p (h n) -> p h n", h=2),
                                             ACT.Square).then_inc(qsq_ready, 1)
                        pend = i
                        i += 1
                if attend:
                    pair_y(pair - 1)

            def pair_y(pair):
                act.wait_ge(o_kept, pair * 8 + 8)
                dst = yh_r[:, bass.ds(pair, 1), :, 0:HP].rearrange("p o h n -> p (o h) n")
                nc.scalar.activation(dst, o32[:].rearrange("p h n -> p (h n)")[:, 0:SEQ]
                                     .rearrange("p (h n) -> p h n", h=2), ACT.Copy).then_inc(yh_ready, 1)

            def bias_load(pair):
                act.dma_start(tb, bias_tab[bass.ds(pair * 2, 2), :, :].rearrange("h p w -> p h w")).then_inc(tb_in, 16)

            def finish(pair):
                bias_load(pair)
                for i in range(3):
                    act.wait_ge(kvt_ready, pair * 7 + 2 * i + 2)
                    nc.scalar.activation(kv_tok[:, i, :, 1, :],
                                         (M, N, M)[i][:, 1, :].rearrange("p (t d) -> p t d", t=4),
                                         ACT.Copy).then_inc(kvt_act, 1)
                act.wait_ge(kvt_dve, pair * 4 + 3)
                act.wait_ge(kvt_act, pair * 3 + 3)
                col = pair * P
                o = p_kv[0].rearrange("l b n k h d -> (l b n) k (h d)")
                act.dma_start(o[:, :, bass.ds(col, P)], kv_tok[:, 0, 3]).then_inc(kv_out, 16)
                for g in (1, 2):
                    o = p_kv[g].rearrange("l b (n c) k h d -> (l b n) c k (h d)", c=NCLS)
                    for c in range(NCLS):
                        act.dma_start(o[:, c, :, bass.ds(col, P)], kv_tok[:, g, c]).then_inc(kv_out, 16)

            ch.begin(0)
            project(0, False)
            ch.end()
            finish(0)
            with act.Fori(1, NP_) as pair:
                ch.begin(pair - 1, 6)
                project(pair, True)
                act.wait_ge(kv_out, pair * (16 * 9))
                finish(pair)
            ch.end(NP_ - 1)
            for n in range(8):
                if n:
                    pt_copy((NP_ - 1) * 8 + n - 1)
                exp_unit((NP_ - 1) * 8 + n)
            pt_copy(NP_ * 8 - 1)
            pair_y(NP_ - 1)

            act.wait_ge(samp, 1)
            act.dma_start(hots[0:NB, 0:NSC], hot_s).then_inc(samp_vin, 16)
            new_rows = [s_kv[g][0, :, KEEP[g] - 1].rearrange("b k h d -> b k (h d)") for g in range(NG)]
            for g in range(NG):
                act.dma_start(new_rows[g], kv_s[:, g]).then_inc(samp_rows, 16)
            act.wait_ge(samp_rows, 16 * NG)
            for g in range(NG):
                act.dma_start(vnew[g:g + 1, :, :], new_rows[g][:, 1, :].rearrange("(o b) n -> o b n", o=1)) \
                    .then_inc(samp_vin, 16)

            def cache_load(n):
                b, kv = n % NS, n // NS
                if n >= NS + 2:
                    act.wait_ge(samp_v, n - 1 - NS)
                elif n >= 2:
                    act.wait_ge(samp_kt, NP_ * (n - 1))
                for g in range(NG):
                    st = GROUPS[g][1]
                    src = caches[g][0, b].rearrange("(n s) k h d -> n s k (h d)", s=st)[:, 0, kv, :]
                    act.dma_start(kvb[0:NBACK[g], n % 2, g, :], src).then_inc(samp_in[n % 2], 16)

            cache_load(0)
            cache_load(1)
            for b in range(NS):
                for q in range(NP_):
                    if (b * NP_ + q) % 2 == 1:
                        act.wait_ge(samp_kt, b * NP_ + q + 1)
                        copy_kt(nc.scalar, b, q, act_engine=True)
                if b + 2 < NS:
                    cache_load(b + 2)
            act.wait_ge(samp_m, 1)
            nc.scalar.activation(se[0:64, 0:NSC], sl[0:64, 0:NSC], ACT.Exp, bias=small[0:64, 4:5], scale=-1.0,
                                 accum_out=small[0:64, 5:6]).then_inc(samp_e, 1)
            for n in range(NS, 2 * NS):
                cache_load(n)
            act.wait_ge(samp_o, 1)
            dst = yh_r[:, 0:NP_, :, HP:HALF]
            nc.scalar.activation(dst, os_.rearrange("p q (h n) -> p q h n", h=2), ACT.Copy).then_inc(yh_ready, 1)

            nc.scalar.preload_act_table(ACT.Copy)
            with act.Fori(0, 2) as it:
                for c in range(4):
                    step(S_WO, it, c)
                    gained(3, it * 4 + c, it * 4 + (c + 3 * DK))
            ch.begin()
            rms(3)
            ch.end()
            ffn(1, S_GU1, S_DN1, 3, DK + FK, DK + FK, 4 * DK, None)

            for t in range(4):
                act.wait_ge(fin_s, t + 1)
                act.dma_start(y_prompt[0, t * P:(t + 1) * P, :], ytok[:, t, :]).then_inc(out_done, 16)
            act.wait_ge(fin_s, 5)
            act.dma_start(y_sample.rearrange("b s n -> (b s) n"), ys_tok).then_inc(out_done, 16)
            act.wait_ge(kv_out, 16 * 9 * NP_)
            act.wait_ge(out_done, OUT_ALL)

        @block.vector
        def _(dve):
            V = nc.vector
            ch = Chain(dve, dve_chain)

            def split_lo(st, it, c):
                dve.wait_ge(hi_done, st.chunk(it, c) + 1)
                V.tensor_tensor(wl[c % 2][:], wraw[:, c % 4], wh[c % 2][:].bitcast(F32),
                                ALU.subtract).then_inc(split_done, 1)

            def splits(st, it, c, last=False):
                if last and c >= st.per_body - 2:
                    return
                for di, cc in ahead(st, c):
                    split_lo(st, it + di, cc)

            def gained(norm, m, n, last=False):
                hm = hh[:, bass.ds(m, 1)].rearrange("p o h n -> p (o h) n").bitcast(F32)
                xm = x[:, bass.ds(m, 1)].rearrange("p o h n -> p (o h) n")
                dve.wait_ge(h_ready, n + 1)
                V.scalar_tensor_tensor(out=hl[:, bass.ds(m, 1)].rearrange("p o h n -> p (o h) n"), in0=xm,
                                       scalar=params[:, bass.ds(m + GAIN[norm], 1)], in1=hm,
                                       op0=ALU.mult, op1=ALU.subtract).then_inc(hl_ready, 1)
                dve.wait_ge(sq_ready, n + 1)
                dve.wait_ge(ssq_ready, n + 1)
                V.tensor_tensor(ssq[:], ssq[:], sq, ALU.add).then_inc(ssq_ready, 1)

            def rms(norm):
                dve.wait_ge(ms_ready, 2 * norm + 1)
                V.tensor_scalar(r[:], N[:, :, 0:HALF], EPS, None, ALU.add).then_inc(ms_ready, 1)
                ch.after(V.memset(ssq[:], 0.0))
                dve.wait_ge(r_ready, norm + 1)

            def residual(st, it, c, par, m, n):
                xm = x[:, bass.ds(m, 1)].rearrange("p o h n -> p (o h) n")
                dve.wait_ge(chunk_used, st.chunk(it, c) + 1)
                V.tensor_tensor(xm, acc[:, par, :, 0:HALF], xm, ALU.add).then_inc(x_ready, 1)
                dve.wait_ge(x_ready, n + 1)
                dve.sem_inc(acc_free, 1)

            def taps(v, f, w1, w2):
                dve.wait_ge(c0_ready, v + 1)
                ch.after(V.scalar_tensor_tensor(out=cv[:], in0=u[:, 1:1 + CO], scalar=params[:, bass.ds(f + w1, 1)],
                                                in1=cv[:], op0=ALU.mult, op1=ALU.add))
                V.scalar_tensor_tensor(out=cv[:], in0=u[:, 2:2 + CO], scalar=params[:, bass.ds(f + w2, 1)],
                                       in1=cv[:], op0=ALU.mult, op1=ALU.add).then_inc(conv_done, 1)

            def y_lo(n, slot):
                dve.wait_ge(yh_ready, n + 1)
                V.tensor_tensor(yl_r[:, bass.ds(slot, 1)].rearrange("p o h n -> p (o h) n"), y32[:],
                                yh[:, bass.ds(slot, 1)].rearrange("p o h n -> p (o h) n"),
                                ALU.subtract).then_inc(yl_ready, 1)
                dve.wait_ge(yl_ready, n + 1)

            V.memset(small[:, 0:1], 0.0).then_inc(split_done, 4)
            V.memset(small[:, 7:8], EPS).then_inc(conv_done, 1)
            V.memset(u[:, 0:2], 0.0).then_inc(rows_kept, 1)
            V.memset(rb[NB:NB + 1, :], 1.0).then_inc(gain_ready, 1)
            V.memset(ssq[:], 0.0).then_inc(ssq_ready, 1)
            dve.wait_ge(setup_t, 1)
            V.tensor_copy(params[:], M[:, 0, 0:NPC])
            V.tensor_copy(hist_sc[:].rearrange("p x f -> p (x f)"), M[:, 1, 0:P])
            V.tensor_copy(hist_ffn[:].rearrange("p l x f -> p l (x f)"), acc[:, 1, :, 0:16 * FK]) \
                .then_inc(params_ready, 1)
            dve.wait_ge(params_ready, 1)
            V.memset(small[:, 0:1], 0.0).then_inc(acc_free, 2)
            dve.wait_ge(gains_in, 64)
            V.tensor_scalar(gq[:, 0:1], gq[:, 0:1], SCALE, None, ALU.mult).then_inc(gain_ready, 1)
            for c in range(2):
                split_lo(S_IN, 0, c)
            for m in range(DK):
                dve.wait_ge(xt_ready, m + 1)
                V.tensor_copy(x[:, m, :, 0:HP], M[:, m % 2, :].rearrange("p (h n) -> p h n", h=2))
                V.tensor_copy(x[:, m, :, HP:HALF], N[:, 0, m * NS:(m + 1) * NS].rearrange("p (h n) -> p h n", h=2)) \
                    .then_inc(x_ready, 1)
                gained(0, m, m)
            dve.wait_ge(vec_mm, 1)
            V.tensor_copy(vec_sb_t[:, 0:1024], acc[0:H, 1].rearrange("p h n -> p (h n)"))
            V.tensor_copy(vec_sb_t[:, 1024:1536], M[0:H, 0, :]).then_inc(vec_sb, 1)
            rms(0)
            ch.end()

            bb, cc_, xx = t1, y32, sv[:, 0:2 * HALF].rearrange("p (h n) -> p h n", h=2)
            with dve.Fori(0, 2) as it:
                ch.begin(it, 12)
                for j in range(4):
                    v = it * 4 + j
                    for c, dst in enumerate((bb[:], cc_[:], xx)):
                        k = 3 * j + c
                        dve.wait_ge(chunk_used, S_IN.chunk(it, k) + 1)
                        V.tensor_tensor(dst, acc[:, k % 2, :, 0:HALF], r[:], ALU.mult).then_inc(acc_free, 1)
                        splits(S_IN, it, k)
                    dve.wait_ge(acc_free, S_IN.tile(it, 3 * j + 2) + 3)
                    dve.wait_ge(rows_kept, v + 1)
                    V.tensor_tensor(u_prompt, prompt(cc_), prompt(xx), ALU.mult)
                    V.tensor_tensor(u_new, sample(cc_), sample(xx), ALU.mult).then_inc(u_ready, 1)
                    dve.wait_ge(u_ready, v + 1)
                    taps(v, v, PC_SCW + DK, PC_SCW + 2 * DK)
                    dve.wait_ge(conv_done, v + 2)
                    ch.after(V.tensor_tensor(prompt(y32), prompt(bb), conv_prompt(cv), ALU.mult))
                    ch.after(V.tensor_tensor(sample(y32), sample(bb), conv_rows(cv), ALU.mult))
                    dve.sem_inc(y_ready, 1)
                    y_lo(v, v)
            ch.end(2)

            def rows_flush(n):
                dve.wait_ge(rows_t, n + 1)
                if n == 0:
                    V.tensor_copy(newh_tok[:, 0:P], N[:, 1, 0:P])
                    V.tensor_copy(newh_tok[0:16, P:2 * P], N[0:16, 1, P:2 * P]).then_inc(rows_tok, 1)
                else:
                    dve.wait_ge(out_done, 16 * (2 + 5 * (n - 1)))
                    nt = 18 * FK // 4
                    V.tensor_copy(newh_tok[0:nt, :], N[0:nt, 1, :]).then_inc(rows_tok, 1)

            rows_flush(0)

            with dve.Fori(0, 2) as it:
                for c in range(4):
                    m = it * 4 + c
                    residual(S_OUT, it, c, c % 2, m, m + DK)
                    splits(S_OUT, it, c)
                    gained(1, m, m + DK)
            ch.begin()
            rms(1)
            ch.end()

            def ffn(layer, gu, dn, v0, x0, next_norm, rows_n):
                pc = PC_L[layer]
                with dve.Fori(0, FK // 2) as it:
                    ch.begin(it, 6)
                    for i in range(2):
                        f = it * 2 + i
                        dve.wait_ge(chunk_used, gu.chunk(it, 2 * i) + 1)
                        dve.wait_ge(rows_kept, f + (v0 + 1))
                        V.tensor_tensor(u_prompt, acc[:, 0, :, 0:HP], prompt(r), ALU.mult)
                        V.tensor_tensor(u_new, acc[:, 0, :, HP:HALF], sample(r), ALU.mult).then_inc(u_ready, 1)
                        dve.wait_ge(u_ready, f + (v0 + 1))
                        dve.sem_inc(acc_free, 1)
                        splits(gu, it, 2 * i)
                        taps(f + v0, f, pc + FK, pc + 2 * FK)
                        dve.wait_ge(silu_ready, f + (layer * FK + 1))
                        V.tensor_tensor(prompt(t1), conv_prompt(sv), prompt(r), ALU.mult)
                        ch.after(V.tensor_tensor(sample(t1), conv_rows(sv), sample(r), ALU.mult))
                        dve.wait_ge(chunk_used, gu.chunk(it, 2 * i + 1) + 1)
                        ch.after(V.tensor_tensor(y32[:], acc[:, 1, :, 0:HALF], t1[:], ALU.mult))
                        dve.sem_inc(acc_free, 1)
                        dve.sem_inc(y_ready, 1)
                        splits(gu, it, 2 * i + 1)
                        y_lo(f + v0 + YOFF[layer], f)
                ch.end(FK // 2)
                rows_flush(rows_n)

                def down(it, last):
                    for c in range(12):
                        if c % 3 < 2:
                            dve.wait_ge(chunk_used, dn.chunk(it, c) + 1)
                            splits(dn, it, c, last)
                        else:
                            m = it * 4 + c // 3
                            residual(dn, it, c, (c // 3) % 2, m, m + x0)
                            splits(dn, it, c, last)
                            if next_norm is not None:
                                gained(next_norm, m, m + x0)
                if next_norm is None:
                    down(0, False)
                    down(1, True)
                else:
                    with dve.Fori(0, 2) as it:
                        down(it, False)
                    ch.begin()
                    rms(next_norm)
                    ch.end()

            ffn(0, S_GU0, S_DN0, DK, 2 * DK, 2, 1)

            def unit_pt(n):
                dve.wait_ge(pt_ready, n + 1)
                V.tensor_copy(PTS[:, 0:512], N[:, 0, :]).then_inc(pt_dve, 1)

            def unit_o(n, h2, cls):
                dve.wait_ge(o_ready, n + 1)
                s = slice(h2 * DH, h2 * DH + DH)
                dst = o32[s].rearrange("p h n -> p (h n)")[:, 0:SEQ].rearrange("p (i c) -> p i c", c=NCLS)[:, :, cls]
                V.tensor_copy(dst, M[s, 0, 0:P]).then_inc(o_kept, 1)

            def unit_softmax(n, h2, cls):
                dve.wait_ge(s_ready, n + 1)
                dve.sem_inc(softmax_steps, 1)
                b0 = NCLS - 1 - cls
                ch.after(V.tensor_tensor_reduce(out=lg[:, 0:512], in0=M[:, 0, :], in1=tb[:, h2, b0:b0 + SEQ],
                                                scale=-1.0, scalar=BIG, op0=ALU.add, op1=ALU.min,
                                                accum_out=small[:, 0:1]))
                dve.sem_inc(softmax_steps, 1)
                V.tensor_tensor_reduce(out=lg[:, 512:768], in0=M[:, 1, 0:256], in1=tb[:, h2, T0W:TBW],
                                       scale=-1.0, scalar=small[:, 0:1], op0=ALU.add, op1=ALU.min,
                                       accum_out=small[:, 1:2]).then_inc(neg_ready, 1)
                dve.wait_ge(e_ready, n + 1)
                ch.after(V.reciprocal(small[:, 3:4], small[:, 2:3]))
                V.tensor_scalar(pr[:], pr[:], small[:, 3:4], None, ALU.mult).then_inc(p_ready, 1)

            def tile_out(pair, c, i):
                g = c // 3
                dve.wait_ge(chunk_used, S_QKV.chunk(pair, c) + 1)
                a = acc[:, c % 2]
                if c % 3 < 2 or g == 0:
                    t = qk_t[:, i] if c % 3 < 2 else v_t[:, 0]
                    V.tensor_tensor(t[:, 0:SEQ].rearrange("p (h n) -> p h n", h=2), a[:, :, 0:HP], prompt(r),
                                    ALU.mult)
                else:
                    t = v_t[:, g]
                    o = t[:, 0:SEQ].rearrange("p (c h n) -> p h n c", c=NCLS, h=2)
                    V.tensor_tensor(o, a[:, :, 0:HP].rearrange("p h (n c) -> p h n c", c=NCLS),
                                    prompt(r).rearrange("p h (n c) -> p h n c", c=NCLS), ALU.mult)
                ch.after(V.tensor_tensor(t[:, SEQ:TT].rearrange("p (h n) -> p h n", h=2), a[:, :, HP:HALF],
                                         sample(r), ALU.mult))
                dve.sem_inc(acc_free, 1)
                if c % 3 < 2:
                    dve.sem_inc(qk_ready, 1)

            def project(pair, attend):
                i = 0
                for c in range(9):
                    n = (pair - 1) * 8
                    if attend and c >= 1:
                        unit_pt(n + c - 1)
                        unit_o(n + c - 1, *UNITS[c - 1])
                    if attend and c < 8:
                        unit_softmax(n + c, *UNITS[c])
                    tile_out(pair, c, i)
                    if c % 3 < 2:
                        i += 1
                    splits(S_QKV, pair, c)
                if attend:
                    pair_y(pair - 1)

            def pair_y(pair):
                dve.wait_ge(yh_ready, pair + (DK + FK + 1))
                dst = yl_r[:, bass.ds(pair, 1), :, 0:HP].rearrange("p o h n -> p (o h) n")
                src = yh[:, bass.ds(pair, 1), :, 0:HP].rearrange("p o h n -> p (o h) n")
                V.tensor_tensor(dst, o32[:].rearrange("p h n -> p (h n)")[:, 0:SEQ]
                                .rearrange("p (h n) -> p h n", h=2), src, ALU.subtract).then_inc(yl_ready, 1)

            def finish(pair):
                dve.wait_ge(inv_ready, pair * 6 + 6)
                for i in range(6):
                    g, isk = i // 2, i % 2
                    o = qka[:, i, 0:SEQ]
                    a, b = qk_t[:, i, 0:SEQ], inv[:, i, 0:SEQ]
                    if not (g == 0 and isk):
                        o = o.rearrange("p (c n) -> p n c", c=NCLS)
                        a = a.rearrange("p (n c) -> p n c", c=NCLS)
                        b = b.rearrange("p (n c) -> p n c", c=NCLS)
                    V.scalar_tensor_tensor(out=o, in0=a, scalar=gq[:, isk:isk + 1], in1=b, op0=ALU.mult,
                                           op1=ALU.mult)
                    dst = (ks if isk else qs)[:, g, bass.ds(pair, 1), :].rearrange("p o n -> p (o n)")
                    V.scalar_tensor_tensor(out=dst, in0=qk_t[:, i, SEQ:TT], scalar=gq[:, isk:isk + 1],
                                           in1=inv[:, i, SEQ:TT], op0=ALU.mult, op1=ALU.mult)
                    V.scalar_tensor_tensor(out=qka[:, i, SEQ:TT], in0=qk_t[:, i, SEQ:TT],
                                           scalar=gq[:, isk:isk + 1], in1=inv[:, i, SEQ:TT], op0=ALU.mult,
                                           op1=ALU.mult).then_inc(norm_ready, 1)
                for i in range(3):
                    dve.wait_ge(kvt_ready, pair * 7 + 2 * i + 1)
                    V.tensor_copy(kv_tok[:, i, :, 0, :],
                                  (M, N, M)[i][:, 0, :].rearrange("p (t d) -> p t d", t=4)).then_inc(kvt_dve, 1)
                dve.wait_ge(kvt_ready, pair * 7 + 7)
                V.tensor_copy(kv_s[:, :, :, bass.ds(pair * P, P)].rearrange("p g k d -> p (g k) d"),
                              acc[0:NS, 1].rearrange("p h (t d) -> p (h t) d", d=P)[:, 0:6, :]) \
                    .then_inc(kvt_dve, 1)

            dve.wait_ge(gain_ready, 2)
            ch.begin()
            project(0, False)
            ch.end()
            finish(0)
            with dve.Fori(1, NP_) as pair:
                ch.begin(pair - 1, 9 + 16)
                project(pair, True)
                dve.wait_ge(kv_out, pair * (16 * 9))
                finish(pair)
            ch.end(NP_ - 1)
            ch.begin()
            for n in range(8):
                if n:
                    unit_pt((NP_ - 1) * 8 + n - 1)
                    unit_o((NP_ - 1) * 8 + n - 1, *UNITS[n - 1])
                unit_softmax((NP_ - 1) * 8 + n, *UNITS[n])
            unit_pt(NP_ * 8 - 1)
            unit_o(NP_ * 8 - 1, *UNITS[7])
            pair_y(NP_ - 1)

            dve.wait_ge(o_ready, NP_ * 8)
            dve.wait_ge(kv_out, 16 * 9 * NP_)
            dve.wait_ge(kvt_dve, 4 * NP_)
            ch.after(V.memset(qblk, 0.0))
            V.tensor_copy(small[:, 6:7], small[:, 7:8]).then_inc(samp, 1)
            for g in range(NG):
                for q in range(NP_):
                    for j in range(2):
                        s = slice(j * DH, j * DH + DH)
                        d = qblk[s, g, q].rearrange("p b m -> p (b m)")
                        a = 2 * q + j
                        last = V.tensor_copy(d[:, a:a + (NS - 1) * 72 + 1:72], qs[s, g, q, :])
            last.then_inc(samp, 1)
            dve.wait_ge(rb_in, 32)
            for b in range(NS):
                last = V.tensor_copy(rbs[0:NB, :, b, :], rb[0:NB, :].rearrange("p (g h) -> p g h", g=NG))
            last.then_inc(samp, 1)
            for b in range(NS):
                for q in range(NP_):
                    if (b * NP_ + q) % 2 == 0:
                        dve.wait_ge(samp_kt, b * NP_ + q + 1)
                        copy_kt(V, b, q, act_engine=False)
            dve.wait_ge(samp_l, 1)
            ch.after(V.tensor_scalar(sl[0:64, 0:NSC], M[0:64, 0, 0:NSC], -1.0, None, ALU.mult))
            V.tensor_reduce(out=small[0:64, 4:5], in_=sl[0:64, 0:NSC], axis=AX_X, op=ALU.min).then_inc(samp_m, 1)
            dve.wait_ge(samp_e, 1)
            ch.after(V.reciprocal(small[0:64, 5:6], small[0:64, 5:6]))
            ch.after(V.tensor_scalar(se[0:64, 0:NSC], se[0:64, 0:NSC], small[0:64, 5:6], None, ALU.mult))
            for g in range(NG):
                c = SCOL[g] + NBACK[g]
                last = V.tensor_copy(snew[0:64, g:g + 1], se[0:64, c:c + 1])
            last.then_inc(samp_p, 1)
            dve.wait_ge(samp_pt, 1)
            V.tensor_copy(pts[:, 0:2, :], M[:, 1, 0:128].rearrange("p (g m) -> p g m", g=2))
            V.tensor_copy(pts[0:64, 2, :], M[0:64, 1, 128:192])
            V.tensor_copy(pts[0:NG, 3, :], M[0:NG, 1, 192:256]).then_inc(samp_pts, 1)
            dve.wait_ge(samp_v, NS)
            oall = N[:, 0, 0:64].rearrange("p (q b j) -> p q b j", q=NP_, j=2)
            for j in range(2):
                s = slice(j * DH, j * DH + DH)
                ch.after(V.tensor_copy(os_[s], oall[s, :, :, j]))
            dve.sem_inc(samp_o, 1)
            dve.wait_ge(yh_ready, DK + FK + NP_ + 1)
            V.tensor_tensor(yl_r[:, 0:NP_, :, HP:HALF], os_.rearrange("p q (h n) -> p q h n", h=2),
                            yh[:, 0:NP_, :, HP:HALF], ALU.subtract).then_inc(yl_ready, 1)
            ch.end()

            with dve.Fori(0, 2) as it:
                for c in range(4):
                    m = it * 4 + c
                    residual(S_WO, it, c, c % 2, m, m + 3 * DK)
                    splits(S_WO, it, c)
                    gained(3, m, m + 3 * DK)
            ch.begin()
            rms(3)
            ch.end()
            ffn(1, S_GU1, S_DN1, DK + FK, 4 * DK, None, 2)

            for j in range(2):
                last = V.tensor_copy(xs_c[:, :, j * HS:(j + 1) * HS], x[:, :, j, HP:HALF])
            last.then_inc(fin_xs, 1)
            for t in range(4):
                dve.wait_ge(fin_t, t + 1)
                V.tensor_copy(ytok[:, t, :].rearrange("p (h n) -> p h n", h=2), (M, N)[t % 2][:]) \
                    .then_inc(fin_s, 1)
            dve.wait_ge(fin_t, 5)
            V.tensor_copy(ys_tok.rearrange("p (h n) -> p h n", h=2), M[0:NS]).then_inc(fin_s, 1)

        @block.tensor
        def _(pe):
            T = nc.tensor

            def transpose(out, in_):
                k = in_.shape[0]
                return T.transpose(out, in_, ident[0:k, 0:k])

            def products(st, it, c, par, nk, xh, xl, k0, first, last, inserts=None, free_d=2):
                g = st.chunk(it, c)
                pe.wait_ge(split_done, g + 5)
                for k in range(nk):
                    if inserts and k in inserts:
                        inserts[k]()
                    for n, (w, a) in enumerate(((wh, xh), (wh, xl), (wl, xh))):
                        for h2 in range(2):
                            ins = T.matmul(acc[:, par, h2, 0:HALF], w[c % 2][:, k, :], a[:, k0 + k, h2, :],
                                           start=(first and k == 0 and n == 0),
                                           stop=(last and k == nk - 1 and n == 2))
                ins.then_inc(chunk_used, 1)

            def free_acc(st, it, t, d=2):
                pe.wait_ge(acc_free, st.tile(it, t) + (3 - d))

            def mean_square(norm):
                pe.wait_ge(ssq_ready, (norm + 1) * DK + 1)
                for h2 in range(2):
                    ins = T.matmul(N[:, h2, 0:HALF], rms_ones[:], ssq[:, h2, :], start=True, stop=True)
                ins.then_inc(ms_ready, 1)

            pe.wait_ge(pool_set, 6)
            pe.wait_ge(rows_in, 16 * 14)
            transpose(M[:, 0, 0:7 * DK], rows[0:7 * DK, 0, :])
            for i in range(2):
                transpose(M[:, 0, PC_L[i]:PC_L[i] + 4 * FK], rows[0:4 * FK, 1 + i, :])
                for j in range(3):
                    n = min(P, 16 * FK - j * P)
                    transpose(acc[:, 1, i, j * P:j * P + n], rows[0:n, 4 + 3 * i + j, :])
            transpose(M[:, 1, 0:P], rows[:, 3, :]).then_inc(setup_t, 1)
            pe.wait_ge(setup_in, 16 * 5)
            for m in range(DK):
                transpose(N[:, 0, m * NS:(m + 1) * NS], xs_in[:, m * P:(m + 1) * P])
            pe.wait_ge(params_ready, 1)
            for m in range(DK):
                if m >= 2:
                    pe.wait_ge(x_ready, m - 1)
                for t in range(4):
                    ins = transpose(M[:, m % 2, t * P:(t + 1) * P], xin[:, t, m * P:(m + 1) * P])
                ins.then_inc(xt_ready, 1)
            pe.wait_ge(rb_in, 32)
            pe.wait_ge(gain_ready, 1)
            pe.wait_ge(x_ready, DK)
            for g, lo, out in ((0, 0, acc[0:H, 1, 0, :]), (0, 512, acc[0:H, 1, 1, :]), (1, V0, M[0:H, 0, 0:256]),
                               (2, V0 + 256, M[0:H, 0, 256:512])):
                w = out.shape[-1]
                ins = T.matmul(out, rb[:, g * H:(g + 1) * H], hotb[:, lo:lo + w], start=True, stop=True)
            ins.then_inc(vec_mm, 1)
            mean_square(0)
            pe.wait_ge(hl_ready, DK)
            pe.wait_ge(vec_sb, 1)

            with pe.Fori(0, 2) as it:
                for c in range(12):
                    free_acc(S_IN, it, c)
                    products(S_IN, it, c, c % 2, DK, hh, hl, 0, True, True)
            pe.wait_ge(rows_kept, DK + 1)
            transpose(N[:, 1, 0:P], newh[:, 0:P])
            transpose(N[0:16, 1, P:2 * P], newh[:, P:P + 16]).then_inc(rows_t, 1)
            pe.wait_ge(yl_ready, DK)
            with pe.Fori(0, 2) as it:
                for c in range(4):
                    free_acc(S_OUT, it, c)
                    products(S_OUT, it, c, c % 2, DK, yh_r, yl_r, 0, True, True)
            pe.wait_ge(rows_tok, 1)
            mean_square(1)

            def ffn(layer, gu, dn, yn, rows_n, hn, next_norm):
                pe.wait_ge(hl_ready, hn)
                with pe.Fori(0, FK // 2) as it:
                    for c in range(4):
                        free_acc(gu, it, c)
                        products(gu, it, c, c % 2, DK, hh, hl, 0, True, True)
                pe.wait_ge(rows_kept, DK + (layer + 1) * FK + 1)
                nt = 18 * FK // 4
                for j in range(4):
                    ins = transpose(N[0:nt, 1, j * P:(j + 1) * P], newh[:, j * nt:(j + 1) * nt])
                ins.then_inc(rows_t, 1)
                pe.wait_ge(yl_ready, yn)
                with pe.Fori(0, 2) as it:
                    for c in range(12):
                        k0, k1 = DN_CUT[c % 3]
                        if c % 3 == 0:
                            free_acc(dn, it, c // 3)
                        products(dn, it, c, (c // 3) % 2, k1 - k0, yh_r, yl_r, k0, c % 3 == 0, c % 3 == 2)
                if next_norm is not None:
                    pe.wait_ge(rows_tok, rows_n + 1)
                    mean_square(next_norm)

            ffn(0, S_GU0, S_DN0, DK + FK, 1, 2 * DK, 2)

            pe.wait_ge(hl_ready, 3 * DK)
            pe.wait_ge(r_ready, 3)

            def unit_logits(n, h2, cls):
                s = slice(h2 * DH, h2 * DH + DH)
                cq = slice(cls * P, (cls + 1) * P)
                T.matmul(M[:, 0, :], qka[s, 0, cq], qka[s, 1, 0:SEQ], start=True, stop=True)
                T.matmul(M[:, 1, 0:P], qka[s, 2, cq], qka[s, 3, cq], start=True, stop=True)
                T.matmul(M[:, 1, P:2 * P], qka[s, 4, cq], qka[s, 5, cq], start=True, stop=True).then_inc(s_ready, 1)

            def unit_transpose(n):
                pe.wait_ge(p_ready, n + 1)
                for j in range(6):
                    ins = transpose(N[:, j // 4, (j % 4) * P:(j % 4 + 1) * P], pr[:, j * P:(j + 1) * P])
                ins.then_inc(pt_ready, 1)

            def unit_values(n, h2, cls):
                pe.wait_ge(pt_act, n + 1)
                pe.wait_ge(pt_dve, n + 1)
                s = slice(h2 * DH, h2 * DH + DH)
                T.matmul(M[s, 0, 0:P], kv_tok[:, 1, cls, 1, s], PTS[:, 512:640], start=True, stop=False)
                T.matmul(M[s, 0, 0:P], kv_tok[:, 2, cls, 1, s], PTS[:, 640:768], start=False, stop=False)
                for t in range(4):
                    lo, hi = 32 * t, min(32 * t + 64, P)
                    ins = T.matmul(M[s, 0, lo:hi], kv_tok[:, 0, t, 1, s], PTS[:, t * P + lo:t * P + hi],
                                   start=False, stop=(t == 3))
                ins.then_inc(o_ready, 1)

            def head_sums(pair, i):
                pe.wait_ge(qsq_ready, pair * 6 + (i + 1))
                for h2 in range(2):
                    ins = T.matmul(N[:, h2, 0:HALF], head_ones[:], sq[:, h2, :], start=True, stop=True)
                ins.then_inc(qms_ready, 1)

            def project(pair, attend):
                i = [0]
                n0 = (pair - 1) * 8
                for c in range(9):
                    ins = {}
                    if attend and c >= 1:
                        def tr(c=c):
                            if c > 1 and (c - 2) % 3 < 2:
                                pe.wait_ge(inv_ready, pair * 6 + i[0])
                            unit_transpose(n0 + c - 1)
                        ins[1] = tr
                        ins[4] = lambda c=c: unit_values(n0 + c - 1, *UNITS[c - 1])
                    if attend and c < 8:
                        def lgts(c=c):
                            if c >= 1:
                                pe.wait_ge(o_kept, n0 + c)
                            unit_logits(n0 + c, *UNITS[c])
                        ins[5] = lgts
                    if c >= 1 and (c - 1) % 3 < 2:
                        def hs():
                            if i[0] > 0:
                                pe.wait_ge(inv_ready, pair * 6 + i[0])
                            head_sums(pair, i[0])
                            i[0] += 1
                        ins[6] = hs
                    free_acc(S_QKV, pair, c, d=1 if c == 0 else 2)
                    products(S_QKV, pair, c, c % 2, DK, hh, hl, 0, True, True, ins)

            def finish(pair):
                pe.wait_ge(acc_free, S_QKV.tile(pair, 8) + 3)
                pe.wait_ge(inv_ready, pair * 6 + 6)
                for g in range(NG):
                    pe.wait_ge(norm_ready, pair * 6 + (2 * g + 2))
                    for kv in range(2):
                        if g == 2:
                            pe.wait_ge(*((kvt_dve, pair * 4 + 1), (kvt_act, pair * 3 + 1))[kv])
                        src = qka[:, 2 * g + 1] if kv == 0 else v_t[:, g]
                        for t in range(4):
                            ins = transpose((M, N, M)[g][:, kv, t * P:(t + 1) * P], src[:, t * P:(t + 1) * P])
                        ins.then_inc(kvt_ready, 1)
                for g in range(NG):
                    for kv in range(2):
                        j = 2 * g + kv
                        src = qka[:, 2 * g + 1] if kv == 0 else v_t[:, g]
                        ins = transpose(acc[0:NS, 1, j // 4, (j % 4) * P:(j % 4 + 1) * P], src[:, SEQ:TT])
                ins.then_inc(kvt_ready, 1)
                pe.wait_ge(kvt_dve, pair * 4 + 4)
                pe.wait_ge(kvt_act, pair * 3 + 3)
                pe.wait_ge(tb_in, (pair + 1) * 16)

            project(0, False)
            finish(0)
            with pe.Fori(1, NP_) as pair:
                project(pair, True)
                pe.wait_ge(o_kept, pair * 8)
                finish(pair)
            n0 = (NP_ - 1) * 8
            for n in range(8):
                if n:
                    unit_transpose(n0 + n - 1)
                    unit_values(n0 + n - 1, *UNITS[n - 1])
                    pe.wait_ge(o_kept, n0 + n)
                unit_logits(n0 + n, *UNITS[n])
            unit_transpose(n0 + 7)
            unit_values(n0 + 7, *UNITS[7])

            pe.wait_ge(o_kept, n0 + 8)
            pe.wait_ge(samp, 3)
            pe.wait_ge(samp_vin, 64)
            for g in range(NG):
                T.matmul(M[0:64, 0, SCOL[g]:SCOL[g] + NBACK[g] + 1], rbs[0:NB, g].rearrange("p b h -> p (b h)"),
                         hots[0:NB, SCOL[g]:SCOL[g] + NBACK[g] + 1], start=(g == 0), stop=False,
                         skip_group_check=True)

            def logits_of(b, q):
                pe.wait_ge(samp_kts[(b * NP_ + q) % 2], (b * NP_ + q) // 2 + 1)
                for g in range(NG):
                    c = slice(SCOL[g], SCOL[g] + NBACK[g] + 1)
                    ins = T.matmul(M[0:64, 0, c], qblk[:, g, q, b, :], kts[:, b % 2, q, c], start=False,
                                   stop=(b == NS - 1 and q == NP_ - 1 and g == NG - 1), skip_group_check=True)
                return ins

            for b in range(NS):
                pe.wait_ge(samp_in[b % 2], 48 * (b // 2 + 1))
                for q in range(NP_):
                    n = b * NP_ + q
                    if n >= 2:
                        logits_of((n - 2) // NP_, (n - 2) % NP_)
                    off = 0
                    for g in range(NG):
                        ins = transpose(acc[:, n % 2, 0, off:off + NBACK[g]],
                                        kvb[0:NBACK[g], b % 2, g, q * P:(q + 1) * P])
                        off += NBACK[g]
                    ins.then_inc(samp_kt, 1)
            for n in range(NS * NP_ - 2, NS * NP_):
                ins = logits_of(n // NP_, n % NP_)
            ins.then_inc(samp_l, 1)
            pe.wait_ge(samp_p, 1)
            transpose(M[:, 1, 0:64], se[0:64, SCOL[0]:SCOL[0] + P])
            transpose(M[:, 1, 64:128], se[0:64, SCOL[1]:SCOL[1] + P])
            transpose(M[0:64, 1, 128:192], se[0:64, SCOL[2]:SCOL[2] + 64])
            transpose(M[0:NG, 1, 192:256], snew[0:64, 0:NG]).then_inc(samp_pt, 1)
            pe.wait_ge(samp_pts, 1)
            for b in range(NS):
                pe.wait_ge(samp_in[b % 2], 48 * ((b + NS) // 2 + 1))
                for q in range(NP_):
                    o = (q * NS + b) * 2
                    m = b * H + 2 * q
                    for g in range(NG):
                        n = NBACK[g]
                        T.matmul(N[:, 0, o:o + 2], kvb[0:n, b % 2, g, q * P:(q + 1) * P], pts[0:n, g, m:m + 2],
                                 start=(g == 0), stop=False)
                    ins = T.matmul(N[:, 0, o:o + 2], vnew[0:NG, b, q * P:(q + 1) * P], pts[0:NG, 3, m:m + 2],
                                   start=False, stop=True)
                ins.then_inc(samp_v, 1)

            pe.wait_ge(yl_ready, DK + FK + NP_ + 1)
            with pe.Fori(0, 2) as it:
                for c in range(4):
                    free_acc(S_WO, it, c, d=1 if c == 0 else 2)
                    products(S_WO, it, c, c % 2, NP_, yh_r, yl_r, 0, True, True)
            mean_square(3)
            ffn(1, S_GU1, S_DN1, DK + 2 * FK + NP_ + 1, 2, 4 * DK, None)

            pe.wait_ge(x_ready, 5 * DK)
            pe.wait_ge(rows_tok, 3)
            for t in range(4):
                if t >= 2:
                    pe.wait_ge(fin_s, t - 1)
                for k in range(DK):
                    ins = transpose((M, N)[t % 2][:, k // 4, (k % 4) * P:(k % 4 + 1) * P],
                                    x[:, k, t // 2, (t % 2) * P:(t % 2 + 1) * P])
                ins.then_inc(fin_t, 1)
            pe.wait_ge(fin_s, 3)
            pe.wait_ge(fin_xs, 1)
            for k in range(DK):
                ins = transpose(M[0:NS, k // 4, (k % 4) * P:(k % 4 + 1) * P], xs_c[:, k, :])
            ins.then_inc(fin_t, 1)


_INS = ['x_prompt', 'x_sample', 'state_sc_conv', 'cache_kv_d1', 'cache_kv_d4', 'cache_kv_d16', 'state_ffn_conv',
        'norm_mix', 'norm_ffn', 'sc_w_in', 'sc_conv_w', 'sc_w_out', 'attn_w_qkv', 'attn_q_norm', 'attn_k_norm',
        'attn_w_out', 'rel_bias', 'ffn_w_gate', 'ffn_w_up', 'ffn_conv_w', 'ffn_conv_b', 'ffn_w_down']
_OUTS = [(1, SEQ, D), (NS, 1, D), (1, 1, 2, D)] + [(1, 1, min(w, SEQ), 2, H, DH) for w, _ in GROUPS] + \
    [(2, 1, 2, FF), (1, NS, 2, D)] + [(1, NS, k, 2, H, DH) for k in KEEP] + [(2, NS, 2, FF)]


def kernel(**inputs):
    import numpy as _np
    import concourse.bacc as _bacc
    from concourse import mybir as _mybir
    from concourse.bass_utils import run_bass_kernel_spmd as _run

    nc = _bacc.Bacc("TRN2", target_bir_lowering=False, num_devices=1)
    given = [(name, inputs[name]) for name in _INS] + [("bias_onehot", bias_onehot()),
                                                       ("sample_onehot", sample_onehot())]
    arrays, args = {}, []
    for name, a in given:
        a = _np.ascontiguousarray(a)
        arrays[f"in_{name}_dram"] = a
        args.append(nc.dram_tensor(f"in_{name}_dram", a.shape, _mybir.dt.from_np(a.dtype), kind="ExternalInput").ap())
    for i, shape in enumerate(_OUTS):
        args.append(nc.dram_tensor(f"out_{i}_dram", shape, F32, kind="ExternalOutput").ap())
    build(nc, *args)
    got = _run(nc, [arrays], core_ids=[0]).results[0]
    return tuple(got[f"out_{i}_dram"] for i in range(len(_OUTS)))
```

```python
import math
from contextlib import ExitStack

import numpy as np

import concourse.bass as bass
from concourse import mybir

F32 = mybir.dt.float32
F32R = mybir.dt.float32r
ALU = mybir.AluOpType
ACT = mybir.ActivationFunctionType
AX_X = mybir.AxisListType.X

P = 128
D = 1024
DK = D // P
SEQ = 512
NS = 8
HALF = 260
HP = SEQ // 2
HS = NS // 2
FF = 2816
FK = FF // P
H = 8
DH = 64
AW = H * DH
NP_ = AW // P
NG = 3
GROUPS = ((128, 1), (512, 4), (2048, 16))
PAST = 1024
KEEP = tuple(min(w, PAST) for w, _ in GROUPS)
NBACK = tuple(min(w, PAST) // d for w, d in GROUPS)
SCOL = (0, NBACK[0], NBACK[0] + NBACK[1])
NEW = (2, 0, 1)
SK = (P, P, NBACK[2] + NG)
NSC = sum(NBACK) + NG
NB = 32
NEG = -1e30
BIG = 3.0e38
EPS = 1e-6
SCALE = DH ** -0.5
NCLS = 4
CW = SEQ + 2 + 3 * NS
CO = CW - 2
T0W = SEQ + NCLS - 1
TBW = T0W + 2 * P
V0 = 1024
VW = V0 + 512

PC_MIX, PC_FFN, PC_SCW = 0, 2 * DK, 4 * DK
PC_L = (7 * DK, 7 * DK + 4 * FK)
NPC = 7 * DK + 8 * FK


def t5_bucket(dist):
    exact = NB // 2
    n = np.asarray(dist, dtype=np.float32)
    large = exact + np.log(np.maximum(n, 1.0) / exact) / math.log(2048 / exact) * (NB - exact)
    large = np.minimum(np.floor(large), NB - 1)
    return np.where(n < exact, n, large).astype(np.int32)


def bias_onehot():
    t = np.zeros((NB + 1, VW), np.float32)
    for g, off, n, top in ((0, 0, V0, SEQ - 1), (1, V0, 256, P - 1), (2, V0 + 256, 256, P - 1)):
        step = (1, 1, NCLS)[g]
        dil = GROUPS[g][1]
        for m in range(n):
            d = top - m
            if d >= 0 and d % step == 0 and d // step <= GROUPS[g][0] // dil:
                t[t5_bucket(dil * (d // step)), off + m] = 1.0
            else:
                t[NB, off + m] = NEG
    return t


def sample_onehot():
    t = np.zeros((NB, NG, NSC), np.float32)
    for g in range(NG):
        for j in range(NBACK[g]):
            t[t5_bucket(GROUPS[g][1] * (NBACK[g] - j)), g, SCOL[g] + j] = 1.0
        t[t5_bucket(0), g, SCOL[2] + NBACK[2] + NEW.index(g)] = 1.0
    return t


class Stage:

    def __init__(self, chunk0, tile0, loads0, per_body, iters, tiles_per_body):
        self.chunk0, self.tile0, self.loads0 = chunk0, tile0, list(loads0)
        self.per_body, self.iters, self.tiles_per_body = per_body, iters, tiles_per_body
        self.slot_per_body = [len(range(s, per_body, 4)) for s in range(4)]
        self.odd = per_body % 2 == 1

    def chunk(self, it, c):
        return it * self.per_body + (self.chunk0 + c)

    def tile(self, it, t):
        return it * self.tiles_per_body + (self.tile0 + t)

    def loads(self, it, c):
        s = c % 4
        return it * (16 * self.slot_per_body[s]) + 16 * (self.loads0[s] + c // 4 + 1)

    def end(self):
        return (self.chunk0 + self.per_body * self.iters, self.tile0 + self.tiles_per_body * self.iters,
                [a + b * self.iters for a, b in zip(self.loads0, self.slot_per_body)])


class Chain:

    def __init__(self, eng, sem):
        self.eng, self.sem, self.base = eng, sem, 0
        self.it, self.per, self.local = 0, 0, 0

    def begin(self, it=0, per=0):
        self.it, self.per, self.local = it, per, 0

    def after(self, ins):
        ins.then_inc(self.sem, 1)
        self.local += 1
        self.eng.wait_ge(self.sem, self.it * self.per + (self.base + self.local))

    def end(self, iters=1):
        assert iters == 1 or self.local == self.per, (self.local, self.per)
        self.base += self.local * iters


def build(nc, x_prompt, x_sample, state_sc, cache1, cache4, cache16, state_ffn, norm_mix, norm_ffn, sc_w_in,
          sc_conv_w, sc_w_out, w_qkv, q_norm, k_norm, attn_w_out, rel_bias, w_gate, w_up, ffn_conv_w, ffn_conv_b,
          w_down, hot, hot_s, y_prompt, y_sample, p_sc, p_kv1, p_kv4, p_kv16, p_ffn, s_sc, s_kv1, s_kv4, s_kv16,
          s_ffn):
    caches = (cache1, cache4, cache16)
    p_kv = (p_kv1, p_kv4, p_kv16)
    s_kv = (s_kv1, s_kv4, s_kv16)
    bias_vec = nc.dram_tensor("bias_vec", (H, VW), F32, kind="Internal").ap()
    new_kv = nc.dram_tensor("new_kv", (NS, NG, 2, AW), F32, kind="Internal").ap()
    new_q = nc.dram_tensor("new_q", (NS, NG, AW), F32, kind="Internal").ap()
    bias_tab = nc.dram_tensor("bias_tab", (H, P, TBW), F32, kind="Internal").ap()

    with ExitStack() as ctx:
        def sb(name, shape, dt=F32):
            return ctx.enter_context(nc.sbuf_tensor(name, shape, dt))

        def sem(name):
            return ctx.enter_context(nc.semaphore(name))

        x = sb("x", [P, DK, 2, HALF])
        with ExitStack() as same:
            hh = same.enter_context(nc.sbuf_tensor("hh", [P, DK, 2, HALF], F32R))
            hl = same.enter_context(nc.sbuf_tensor("hl", [P, DK, 2, HALF], F32R))
        held = sb("held", [P, 2 * DK * 2 * HALF])
        r = sb("r", [P, 2, HALF])
        ssq = sb("ssq", [P, 2, HALF])
        wraw = sb("wraw", [P, 4, DK, P])
        wh = [sb(f"wh{s}", [P, DK, P], F32R) for s in range(2)]
        wl = [sb(f"wl{s}", [P, DK, P], F32R) for s in range(2)]
        u = sb("u", [P, CW])
        cv = sb("cv", [P, CO])
        sv = sb("sv", [P, CO])
        sq = sv[:, 0:2 * HALF].rearrange("p (h n) -> p h n", h=2)
        y32 = sb("y32", [P, 2, HALF])
        t1 = sb("t1", [P, 2, HALF])
        params = sb("params", [P, NPC])
        hist_sc = sb("hist_sc", [P, 16, DK])
        hist_ffn = sb("hist_ffn", [P, 2, 16, FK])
        newh = sb("newh", [P, 18 * FK])
        newh_tok = sb("newh_tok", [P, 4 * P])
        ident = sb("ident", [P, P])
        rms_ones = sb("rms_ones", [P, P])
        head_ones = sb("head_ones", [P, P])
        gq = sb("gq", [P, 2])
        small = sb("small", [P, 8])
        ACTB = 2 * FK * 2 * HALF
        with ExitStack() as same:
            yh_r = same.enter_context(nc.sbuf_tensor("yh", [P, FK, 2, HALF], F32R))[:]
            yl_r = same.enter_context(nc.sbuf_tensor("yl", [P, FK, 2, HALF], F32R))[:]
        big = sb("big", [P, ACTB])
        yh = yh_r.bitcast(F32)
        NYT = NP_
        pos = [NYT * 2 * HALF]

        def attn(cols):
            o = pos[0]
            if o < FK * 2 * HALF < o + cols:
                o = (FK + NYT) * 2 * HALF
            pos[0] = o + cols
            assert pos[0] <= ACTB, pos[0]
            return big[:, o:o + cols]

        TT = SEQ + NS
        qk_t = attn(6 * TT).rearrange("p (t n) -> p t n", t=6)
        v_t = attn(3 * TT).rearrange("p (t n) -> p t n", t=3)
        qka = attn(6 * TT).rearrange("p (t n) -> p t n", t=6)
        tb = attn(2 * TBW).rearrange("p (j n) -> p j n", j=2)
        pos[0] = (FK + NYT) * 2 * HALF
        inv = attn(6 * TT).rearrange("p (t n) -> p t n", t=6)
        lg = attn(6 * P)
        pr = attn(6 * P)
        kv_tok = attn(NG * 4 * 2 * P).rearrange("p (g t k d) -> p g t k d", g=NG, t=4, k=2)
        o32 = t1
        q_s = attn(NG * AW).rearrange("p (g n) -> p g n", g=NG)
        kv_s = sb("kv_s", [NS, NG, 2, AW])
        rb = sb("rb", [NB + 1, NG * H])
        pt_last = sb("pt_last", [P, 2 * P])

        acc = ctx.enter_context(nc.psum_tensor("acc", [P, 2, 2, 512], F32))
        M = ctx.enter_context(nc.psum_tensor("M", [P, 2, 512], F32))
        N = ctx.enter_context(nc.psum_tensor("N", [P, 2, 512], F32))

        chunk_loaded = [sem(f"chunk_loaded{s}") for s in range(4)]
        hi_done = sem("hi_done")
        split_done = sem("split_done")
        chunk_used = sem("chunk_used")
        acc_free = sem("acc_free")
        dve_chain = sem("dve_chain")
        act_chain = sem("act_chain")
        setup_in = sem("setup_in")
        rows_in = sem("rows_in")
        gains_in = sem("gains_in")
        rb_in = sem("rb_in")
        pool_set = sem("pool_set")
        setup_t = sem("setup_t")
        params_ready = sem("params_ready")
        gain_ready = sem("gain_ready")
        xt_ready = sem("xt_ready")
        x_ready = sem("x_ready")
        h_ready = sem("h_ready")
        sq_ready = sem("sq_ready")
        hl_ready = sem("hl_ready")
        ssq_ready = sem("ssq_ready")
        ms_ready = sem("ms_ready")
        r_ready = sem("r_ready")
        u_ready = sem("u_ready")
        c0_ready = sem("c0_ready")
        rows_kept = sem("rows_kept")
        conv_done = sem("conv_done")
        silu_ready = sem("silu_ready")
        y_ready = sem("y_ready")
        yh_ready = sem("yh_ready")
        yl_ready = sem("yl_ready")
        rows_t = sem("rows_t")
        rows_tok = sem("rows_tok")
        vec_mm = sem("vec_mm")
        vec_sb = sem("vec_sb")
        vec_out = sem("vec_out")
        tab_out = sem("tab_out")
        tb_in = sem("tb_in")
        qk_ready = sem("qk_ready")
        qsq_ready = sem("qsq_ready")
        qms_ready = sem("qms_ready")
        inv_ready = sem("inv_ready")
        norm_ready = sem("norm_ready")
        s_ready = sem("s_ready")
        softmax_steps = sem("softmax_steps")
        neg_ready = sem("neg_ready")
        e_ready = sem("e_ready")
        p_ready = sem("p_ready")
        pt_ready = sem("pt_ready")
        pt_act = sem("pt_act")
        pt_dve = sem("pt_dve")
        o_ready = sem("o_ready")
        o_kept = sem("o_kept")
        kvt_ready = sem("kvt_ready")
        kvt_act = sem("kvt_act")
        kvt_dve = sem("kvt_dve")
        kv_out = sem("kv_out")
        samp_const = sem("samp_const")
        samp_rb = sem("samp_rb")
        samp_rows = sem("samp_rows")
        samp_in = [sem(f"samp_in{i}") for i in range(2)]
        samp_prod = sem("samp_prod")
        samp_lt = sem("samp_lt")
        samp_vin = sem("samp_vin")
        samp_l = sem("samp_l")
        samp_m = sem("samp_m")
        samp_e = sem("samp_e")
        samp_p = sem("samp_p")
        samp_pt = sem("samp_pt")
        samp_pts = sem("samp_pts")
        samp_v = sem("samp_v")
        samp_rows_o = sem("samp_rows_o")
        samp_heads = sem("samp_heads")
        samp_o = sem("samp_o")
        fin_t = sem("fin_t")
        fin_s = sem("fin_s")
        fin_xs = sem("fin_xs")
        out_done = sem("out_done")
        copied = sem("copied")

        stages, at = [], (0, 0, [0] * 4)
        for per_body, iters, tiles in ((12, 2, 12), (4, 2, 4), (4, FK // 2, 4), (12, 2, 4),
                                       (9, NP_, 9), (4, 2, 4), (4, FK // 2, 4), (12, 2, 4)):
            stages.append(Stage(*at, per_body, iters, tiles))
            at = stages[-1].end()
        S_IN, S_OUT, S_GU0, S_DN0, S_QKV, S_WO, S_GU1, S_DN1 = stages
        DN_CUT = ((0, 8), (8, 15), (15, 22))

        def split_tiles(st, c):
            return NP_ if st is S_WO and c >= 2 else DK

        def kmajor(w):
            return w.rearrange("(k p) n -> p k n", p=P)

        SW = NG * AW

        def slot(o):
            return big[:, o:o + SW].rearrange("p (g n) -> p g n", g=NG)

        A0, B0 = NYT * 2 * HALF, (FK + NYT) * 2 * HALF
        skey = [slot(A0), slot(A0 + SW)]
        sq_b = [slot(A0 + 2 * SW), slot(B0)]
        sprod = slot(B0 + SW)
        sval = [held[:, i * SW:(i + 1) * SW].rearrange("p (g n) -> p g n", g=NG) for i in range(5)] + \
            [skey[0], sq_b[0], skey[1]]
        PT = (lg[:, 0:4 * P], lg[:, 4 * P:6 * P])
        PT_LAST = (held[:, 5 * SW:5 * SW + 4 * P], pt_last[:])
        sl, lt = u[:, 2:2 + NSC], u[:, 2 + NSC:2 + NSC + 3 * 64].rearrange("p (g m) -> p g m", g=NG)
        se = cv[:, 0:NSC]
        W = NS * H
        pts = qka.rearrange("p t n -> p (t n)")[:, 0:NG * NS * (W + H)].rearrange("p (g w) -> p g w", g=NG)
        o_rows = pr[0:W, 0:AW]
        rbs = sv[:, 0:3 * 64].rearrange("p (g b h) -> p g b h", g=NG, b=NS)
        hots = [sv[0:NB, 192:192 + NSC], y32[0:NB].rearrange("p h n -> p (h n)")[:, 0:NSC],
                newh[0:NB, 32:32 + NSC]]
        os_ = newh[:, 0:NP_ * NS].rearrange("p (q b) -> p q b", q=NP_)

        xin = big[:, 0:4 * D].rearrange("p (t n) -> p t n", t=4)
        xs_in = big[0:NS, 4 * D:5 * D]
        rows = big[:, 5 * D:5 * D + 10 * P].rearrange("p (t n) -> p t n", t=10)
        hotb = big[0:NB + 1, 5 * D + 10 * P:5 * D + 10 * P + VW]
        vec_sb_t = big[0:H, 8 * D:8 * D + VW]
        ytok = big[:, 0:4 * D].rearrange("p (s n) -> p s n", s=4)
        xs_c = big[:, 4 * D:4 * D + DK * NS].rearrange("p (k n) -> p k n", k=DK)
        ys_tok = big[0:NS, 5 * D:6 * D]

        block = ctx.enter_context(nc.Block())

        @block.sync
        def _(sp):
            def load(st, it, c, w, k0, k1, col):
                g = st.chunk(it, c)
                sp.wait_ge(split_done, g + (4 if c == 0 and (st is S_QKV or (st is S_WO and it == 0)) else 1))
                sp.dma_start(wraw[:, c % 4, 0:k1 - k0, :], w[:, k0:k1, bass.ds(col, P)]) \
                    .then_inc(chunk_loaded[c % 4], 16)

            w = kmajor(sc_w_in[0])
            with sp.Fori(0, 2) as it:
                for c in range(12):
                    load(S_IN, it, c, w, 0, DK, it * (4 * P) + (c % 3) * D + (c // 3) * P)
            w = kmajor(sc_w_out[0])
            with sp.Fori(0, 2) as it:
                for c in range(4):
                    load(S_OUT, it, c, w, 0, DK, it * (4 * P) + c * P)

            def ffn(layer, gu, dn):
                wg, wu, wd = kmajor(w_gate[layer]), kmajor(w_up[layer]), kmajor(w_down[layer])
                with sp.Fori(0, FK // 2) as it:
                    for c in range(4):
                        load(gu, it, c, (wg, wu)[c % 2], 0, DK, it * (2 * P) + (c // 2) * P)
                with sp.Fori(0, 2) as it:
                    for c in range(12):
                        load(dn, it, c, wd, *DN_CUT[c % 3], it * (4 * P) + (c // 3) * P)

            ffn(0, S_GU0, S_DN0)
            w = kmajor(w_qkv[0])
            with sp.Fori(0, NP_) as it:
                for c in range(9):
                    load(S_QKV, it, c, w, 0, DK, it * P + c * AW)
            wo = kmajor(attn_w_out[0])
            for c in range(4):
                load(S_WO, 0, c, wo, 0, NP_, c * P)
            def cache_load(b, kv, dst, done):
                for g in range(NG):
                    src = caches[g][0, b].rearrange("(n s) k h d -> n s k (h d)", s=GROUPS[g][1])[:, 0, kv, :]
                    sp.dma_start(dst[0:NBACK[g], g, :], src).then_inc(done, 16)
                sp.dma_start(dst[NBACK[2]:SK[2], 2, :], new_kv[b, :, kv, :]).then_inc(done, 16)

            sp.wait_ge(samp_rows, 16 * 3)
            for b in range(NS):
                if b >= 2:
                    sp.wait_ge(samp_prod, b - 1)
                cache_load(b, 0, skey[b % 2], samp_in[b % 2])
                q = new_q[b:b + 1]
                for g in range(2):
                    sp.dma_start(sq_b[b % 2][:, g, :], q[:, g, :].partition_broadcast(P)
                                 .rearrange("p o n -> p (o n)")).then_inc(samp_in[b % 2], 16)
                sp.dma_start(sq_b[b % 2][0:NBACK[2] + 1, 2, :], q[:, 2, :].partition_broadcast(NBACK[2] + 1)
                             .rearrange("p o n -> p (o n)")).then_inc(samp_in[b % 2], 16)
                sp.dma_start(sq_b[b % 2][NBACK[2] + 1:SK[2], 2, :], new_q[b, 0:2, :]).then_inc(samp_in[b % 2], 16)
                if b == 0:
                    sp.wait_ge(chunk_used, S_WO.chunk0)
                if b < 5:
                    cache_load(b, 1, sval[b], samp_vin)
            for b in range(5, NS):
                sp.wait_ge(samp_prod, NS - 1 if b < NS - 1 else NS)
                cache_load(b, 1, sval[b], samp_vin)

            for c in range(4):
                load(S_WO, 1, c, wo, 0, NP_, (4 + c) * P)
            ffn(1, S_GU1, S_DN1)

        @block.gpsimd
        def _(pool):
            pool.memset(ident[:], 0.0).then_inc(pool_set, 1)
            pool.memset(rms_ones[:], 1.0 / D).then_inc(pool_set, 1)
            pool.memset(head_ones[:], 0.0).then_inc(pool_set, 1)
            pool.wait_ge(pool_set, 3)
            pool.affine_select(out=ident[:], in_=ident[:], compare_op=ALU.not_equal, fill=1.0, base=0,
                               pattern=[[-1, P]], channel_multiplier=1).then_inc(pool_set, 1)
            for i in range(2):
                pool.wait_ge(pool_set, 4 + i)
                s = slice(i * DH, i * DH + DH)
                pool.memset(head_ones[s, s], 1.0 / DH).then_inc(pool_set, 1)

            flat_in = [c.rearrange("l b n k h d -> (l b) (n k h d)") for c in caches]
            flat_out = [c.rearrange("l b n k h d -> (l b) (n k h d)") for c in s_kv]
            row = 2 * AW
            plan = [(2, (KEEP[2] - 1) // 3, 3, 352), (1, KEEP[1] - 1, 1, 512), (0, KEEP[0] - 1, 1, 128)]
            with pool.Fori(0, NS) as b:
                n = 0
                for g, rows, pieces, desc in plan:
                    for i in range(pieces):
                        pool.wait_ge(chunk_used, b * 24 + (8 + 5 * n))
                        n += 1
                        lo = i * rows * row
                        pool.dma_start(
                            flat_out[g][bass.ds(b, 1), lo:lo + rows * row].rearrange("o (a c) -> (o a) c", a=desc),
                            flat_in[g][bass.ds(b, 1), lo + row:lo + row + rows * row]
                            .rearrange("o (a c) -> (o a) c", a=desc)).then_inc(copied, 16)
            pool.wait_ge(copied, 16 * NS * 5)

        GAIN = (PC_MIX, PC_FFN, PC_MIX + DK, PC_FFN + DK)

        def ahead(st, c):
            if not st.odd:
                return [((c + 2) // st.per_body, (c + 2) % st.per_body)]
            if c == st.per_body - 2:
                return []
            if c == st.per_body - 1:
                return [(1, 0), (1, 1)]
            return [(0, c + 2)]

        def prompt(a):
            return a[:, :, 0:HP]

        def sample(a):
            return a[:, :, HP:HALF]

        u_prompt = u[:, 2:2 + SEQ].rearrange("p (h n) -> p h n", h=2)
        u_rows = u[:, 2 + SEQ:CW].rearrange("p (b w) -> p b w", w=3)
        u_new = u_rows[:, :, 2].rearrange("p (h n) -> p h n", h=2)

        def conv_rows(a):
            return a[:, SEQ + 2:CO:3].rearrange("p (h n) -> p h n", h=2)

        def conv_prompt(a):
            return a[:, 0:SEQ].rearrange("p (h n) -> p h n", h=2)

        UNITS = [(hh_, c) for hh_ in range(2) for c in range(NCLS)]

        OUT_ALL = 16 * (2 + 2 * 5 + NG + 5)

        YOFF = (0, NP_ + 1)

        @block.scalar
        def _(act):
            ch = Chain(act, act_chain)
            for t in range(4):
                act.dma_start(xin[:, t, :], x_prompt[0, t * P:(t + 1) * P, :]).then_inc(setup_in, 16)
            act.dma_start(xs_in, x_sample.rearrange("b s n -> (b s) n")).then_inc(setup_in, 16)
            act.dma_start(rows[0:2 * DK, 0, :], norm_mix.rearrange("l (k p) -> (l k) p", p=P)).then_inc(rows_in, 16)
            act.dma_start(rows[2 * DK:4 * DK, 0, :], norm_ffn.rearrange("l (k p) -> (l k) p", p=P)) \
                .then_inc(rows_in, 16)
            act.dma_start(rows[4 * DK:7 * DK, 0, :], sc_conv_w.rearrange("l j (k p) -> (l j k) p", p=P)) \
                .then_inc(rows_in, 16)
            for i in range(2):
                act.dma_start(rows[0:3 * FK, 1 + i, :], ffn_conv_w[i].rearrange("j (k p) -> (j k) p", p=P)) \
                    .then_inc(rows_in, 16)
                act.dma_start(rows[3 * FK:4 * FK, 1 + i, :],
                              ffn_conv_b[i:i + 1, :].rearrange("o (k p) -> (o k) p", p=P)).then_inc(rows_in, 16)
            act.dma_start(rows[:, 3, :], state_sc.rearrange("l b w (k p) -> (l b w k) p", p=P)).then_inc(rows_in, 16)
            for i in range(2):
                hr = state_ffn[i].rearrange("b w (k p) -> (b w k) p", p=P)
                for j in range(3):
                    n = min(P, 16 * FK - j * P)
                    act.dma_start(rows[0:n, 4 + 3 * i + j, :], hr[j * P:j * P + n, :]).then_inc(rows_in, 16)
            for i in range(2):
                act.dma_start(gq[i * DH:(i + 1) * DH, 0:1], q_norm.rearrange("o d -> d o")).then_inc(gains_in, 16)
                act.dma_start(gq[i * DH:(i + 1) * DH, 1:2], k_norm.rearrange("o d -> d o")).then_inc(gains_in, 16)
            act.dma_start(rb[0:NB, :], rel_bias).then_inc(rb_in, 16)
            act.dma_start(hotb, hot).then_inc(rb_in, 16)

            def split_hi(st, it, c):
                k = split_tiles(st, c)
                act.wait_ge(chunk_loaded[c % 4], st.loads(it, c))
                nc.scalar.activation(wh[c % 2][:, 0:k], wraw[:, c % 4, 0:k], ACT.Copy).then_inc(hi_done, 1)

            def step(st, it, c, last=False):
                g = st.chunk(it, c)
                act.wait_ge(chunk_used, g + 1)
                if last and c >= st.per_body - 2:
                    return
                for di, cc in ahead(st, c):
                    split_hi(st, it + di, cc)

            def gained(norm, m, n):
                act.wait_ge(x_ready, n + 1)
                c = GAIN[norm]
                act.wait_ge(ssq_ready, n + 1)
                nc.scalar.activation(hh[:, bass.ds(m, 1)], x[:, bass.ds(m, 1)], ACT.Copy,
                                     scale=params[:, bass.ds(m + c, 1)]).then_inc(h_ready, 1)
                nc.scalar.activation(sq, x[:, bass.ds(m, 1)].rearrange("p o h n -> p (o h) n"),
                                     ACT.Square).then_inc(sq_ready, 1)

            def rms(norm):
                act.wait_ge(ms_ready, 2 * norm + 2)
                ch.after(nc.scalar.activation(r[:], r[:], ACT.Ln))
                nc.scalar.activation(r[:], r[:], ACT.Exp, scale=-0.5).then_inc(r_ready, 1)

            def conv_act(v, f, hist, keep, nk, wcol, bcol):
                act.wait_ge(conv_done, v + 1)
                act.wait_ge(rows_kept, v + 1)
                ch.after(nc.scalar.activation(u_rows[:, :, 0:2],
                                              hist[:, :, bass.ds(f, 1)].rearrange("p (b w) o -> p b (w o)", w=2),
                                              ACT.Copy))
                act.wait_ge(u_ready, v + 1)
                if bcol is None:
                    nc.scalar.activation(cv[:], u[:, 0:CO], ACT.Copy,
                                         scale=params[:, bass.ds(f + wcol, 1)]).then_inc(c0_ready, 1)
                else:
                    nc.scalar.activation(cv[:], u[:, 0:CO], ACT.Identity, bias=params[:, bass.ds(f + bcol, 1)],
                                         scale=params[:, bass.ds(f + wcol, 1)]).then_inc(c0_ready, 1)
                k = newh[:, 0:18 * nk].rearrange("p (x f) -> p x f", f=nk)[:, :, bass.ds(f, 1)]
                nc.scalar.activation(k[:, 0:16].rearrange("p (b w) o -> p b (w o)", w=2), u_rows[:, :, 1:3], ACT.Copy)
                nc.scalar.activation(k[:, 16:18].rearrange("p w o -> p (w o)"), u[:, SEQ:SEQ + 2],
                                     ACT.Copy).then_inc(rows_kept, 1)

            def y_hi(n, slot):
                act.wait_ge(y_ready, n + 1)
                nc.scalar.activation(yh_r[:, bass.ds(slot, 1)].rearrange("p o h n -> p (o h) n"), y32[:],
                                     ACT.Copy).then_inc(yh_ready, 1)

            act.wait_ge(params_ready, 1)
            nc.scalar.preload_act_table(ACT.Copy)
            for c in range(2):
                split_hi(S_IN, 0, c)
            for m in range(DK):
                gained(0, m, m)
            act.wait_ge(vec_sb, 1)
            act.dma_start(bias_vec, vec_sb_t).then_inc(vec_out, 16)
            rms(0)
            ch.end()

            nc.scalar.preload_act_table(ACT.Silu)
            with act.Fori(0, 2) as it:
                ch.begin(it, 4)
                for j in range(4):
                    for c in range(3):
                        step(S_IN, it, 3 * j + c)
                    v = it * 4 + j
                    conv_act(v, v, hist_sc, newh, DK, PC_SCW, None)
                    y_hi(v, v)
            ch.end(2)
            act.wait_ge(rows_tok, 1)
            act.dma_start(s_sc.rearrange("l b w (k p) -> (l b w k) p", p=P), newh_tok[:, 0:P]).then_inc(out_done, 16)
            act.dma_start(p_sc.rearrange("l b w (k p) -> (l b w k) p", p=P), newh_tok[0:16, P:2 * P]) \
                .then_inc(out_done, 16)

            def ffn(layer, gu, dn, norm, v0, y0, x0, next_norm):
                nc.scalar.preload_act_table(ACT.Silu)
                pc = PC_L[layer]
                with act.Fori(0, FK // 2) as it:
                    ch.begin(it, 2)
                    for i in range(2):
                        f = it * 2 + i
                        step(gu, it, 2 * i)
                        conv_act(f + v0, f, hist_ffn[:, layer], newh, FK, pc, pc + 3 * FK)
                        act.wait_ge(conv_done, f + (v0 + 2))
                        nc.scalar.activation(sv[:], cv[:], ACT.Silu).then_inc(silu_ready, 1)
                        step(gu, it, 2 * i + 1)
                        y_hi(f + y0, f)
                ch.end(FK // 2)
                rows_out(layer)

                def down(it, last):
                    for c in range(12):
                        step(dn, it, c, last)
                        if c % 3 == 2 and next_norm is not None:
                            m = it * 4 + c // 3
                            gained(next_norm, m, m + x0)
                if next_norm is None:
                    down(0, False)
                    down(1, True)
                else:
                    with act.Fori(0, 2) as it:
                        down(it, False)
                    ch.begin()
                    rms(next_norm)
                    ch.end()

            def rows_out(layer):
                act.wait_ge(rows_tok, layer + 2)
                srows = s_ffn[layer].rearrange("b w (k p) -> (b w k) p", p=P)
                prows = p_ffn[layer].rearrange("b w (k p) -> (b w k) p", p=P)
                ns, nt = 16 * FK, 18 * FK // 4
                for j in range(4):
                    lo, hi = j * nt, (j + 1) * nt
                    if lo < ns:
                        n = min(hi, ns) - lo
                        act.dma_start(srows[lo:lo + n, :], newh_tok[0:n, j * P:(j + 1) * P]).then_inc(out_done, 16)
                    if hi > ns:
                        a = max(lo, ns)
                        act.dma_start(prows[a - ns:hi - ns, :], newh_tok[a - lo:nt, j * P:(j + 1) * P]) \
                            .then_inc(out_done, 16)

            act.wait_ge(vec_out, 16)
            for off, step_, w, dst in ((NCLS * (P - 1), NCLS, T0W, 0), (V0 + P - 1, 1, P, T0W),
                                       (V0 + 256 + P - 1, 1, P, T0W + P)):
                act.dma_start(bias_tab[:, :, dst:dst + w],
                              bass.AP(bias_vec.tensor, off, [[VW, H], [-step_, P], [1, w]])).then_inc(tab_out, 16)
            with act.Fori(0, 2) as it:
                for c in range(4):
                    step(S_OUT, it, c)
                    gained(1, it * 4 + c, it * 4 + (c + DK))
            ch.begin()
            rms(1)
            ch.end()
            ffn(0, S_GU0, S_DN0, 1, DK, DK, 2 * DK, 2)

            act.wait_ge(tab_out, 48)
            nc.scalar.preload_act_table_set("natural_log_exp_and_others")

            def exp_unit(n):
                act.wait_ge(neg_ready, n + 1)
                nc.scalar.activation(pr[:], lg[:], ACT.Exp, bias=small[:, 1:2], scale=-1.0,
                                     accum_out=small[:, 2:3]).then_inc(e_ready, 1)

            def pt_copy(n, pt=PT):
                act.wait_ge(pt_ready, n + 1)
                nc.scalar.activation(pt[1], N[:, 1, 0:256], ACT.Copy).then_inc(pt_act, 1)

            def head_rms(pair, i):
                q = pair * 6 + i
                act.wait_ge(qms_ready, q + 1)
                t = inv[:, i, :].rearrange("p (h n) -> p h n", h=2)
                ch.after(nc.scalar.activation(t, N[:, :, 0:HALF], ACT.Ln, bias=small[:, 7:8]))
                nc.scalar.activation(t, t, ACT.Exp, scale=-0.5).then_inc(inv_ready, 1)

            def project(pair, attend):
                i = 0
                pend = None
                for c in range(9):
                    if attend and c >= 1:
                        pt_copy((pair - 1) * 8 + c - 1)
                    if pend is not None:
                        head_rms(pair, pend)
                        pend = None
                    if attend and c < 8:
                        exp_unit((pair - 1) * 8 + c)
                    if c < 8:
                        step(S_QKV, pair, c)
                    if c % 3 < 2:
                        q = pair * 6 + i
                        act.wait_ge(qk_ready, q + 1)
                        nc.scalar.activation(sq, qk_t[:, i, :].rearrange("p (h n) -> p h n", h=2),
                                             ACT.Square).then_inc(qsq_ready, 1)
                        pend = i
                        i += 1
                if attend:
                    pair_y(pair - 1)

            def pair_y(pair):
                act.wait_ge(o_kept, pair * 8 + 8)
                dst = yh_r[:, bass.ds(pair, 1), :, 0:HP].rearrange("p o h n -> p (o h) n")
                nc.scalar.activation(dst, o32[:].rearrange("p h n -> p (h n)")[:, 0:SEQ]
                                     .rearrange("p (h n) -> p h n", h=2), ACT.Copy).then_inc(yh_ready, 1)

            def bias_load(pair):
                act.dma_start(tb, bias_tab[bass.ds(pair * 2, 2), :, :].rearrange("h p w -> p h w")).then_inc(tb_in, 16)

            def finish(pair):
                act.wait_ge(chunk_used, S_QKV.chunk(pair, 8) + 1)
                split_hi(S_QKV, pair + 1, 0)
                bias_load(pair)
                for i in range(3):
                    if i == 2:
                        split_hi(S_QKV, pair + 1, 1)
                    act.wait_ge(kvt_ready, pair * 7 + 2 * i + 2)
                    nc.scalar.activation(kv_tok[:, i, :, 1, :],
                                         (M, N, M)[i][:, 1, :].rearrange("p (t d) -> p t d", t=4),
                                         ACT.Copy).then_inc(kvt_act, 1)
                act.wait_ge(kvt_dve, pair * 4 + 3)
                act.wait_ge(kvt_act, pair * 3 + 3)
                col = pair * P
                o = p_kv[0].rearrange("l b n k h d -> (l b n) k (h d)")
                act.dma_start(o[:, :, bass.ds(col, P)], kv_tok[:, 0, 3]).then_inc(kv_out, 16)
                for g in (1, 2):
                    o = p_kv[g].rearrange("l b (n c) k h d -> (l b n) c k (h d)", c=NCLS)
                    for c in range(NCLS):
                        act.dma_start(o[:, c, :, bass.ds(col, P)], kv_tok[:, g, c]).then_inc(kv_out, 16)

            ch.begin(0)
            project(0, False)
            ch.end()
            finish(0)
            with act.Fori(1, NP_) as pair:
                ch.begin(pair - 1, 6)
                project(pair, True)
                act.wait_ge(kv_out, pair * (16 * 9))
                finish(pair)
            ch.end(NP_ - 1)
            act.wait_ge(kvt_dve, 4 * NP_)
            for g in range(NG):
                act.dma_start(hots[g], hot_s[:, g, :]).then_inc(samp_const, 16)
            act.dma_start(new_kv[:, 0], kv_s[:, 2]).then_inc(samp_rows, 16)
            act.dma_start(new_kv[:, 1:3], kv_s[:, 0:2]).then_inc(samp_rows, 16)
            act.dma_start(new_q, q_s[0:NS]).then_inc(samp_rows, 16)
            for g in range(NG):
                act.dma_start(s_kv[g][0, :, KEEP[g] - 1].rearrange("b k h d -> b k (h d)"), kv_s[:, g]) \
                    .then_inc(out_done, 16)
            for n in range(8):
                if n:
                    pt_copy((NP_ - 1) * 8 + n - 1, PT_LAST)
                exp_unit((NP_ - 1) * 8 + n)
            pt_copy(NP_ * 8 - 1, PT_LAST)
            pair_y(NP_ - 1)

            act.wait_ge(samp_m, 1)
            nc.scalar.activation(se[0:64], sl[0:64], ACT.Exp, bias=small[0:64, 4:5], scale=-1.0,
                                 accum_out=small[0:64, 5:6]).then_inc(samp_e, 1)
            act.wait_ge(samp_o, 1)
            dst = yh_r[:, 0:NP_, :, HP:HALF]
            nc.scalar.activation(dst, os_.rearrange("p q (h n) -> p q h n", h=2), ACT.Copy).then_inc(yh_ready, 1)

            nc.scalar.preload_act_table(ACT.Copy)
            with act.Fori(0, 2) as it:
                for c in range(4):
                    step(S_WO, it, c)
                    gained(3, it * 4 + c, it * 4 + (c + 3 * DK))
            ch.begin()
            rms(3)
            ch.end()
            ffn(1, S_GU1, S_DN1, 3, DK + FK, DK + FK, 4 * DK, None)

            for t in range(4):
                act.wait_ge(fin_s, t + 1)
                act.dma_start(y_prompt[0, t * P:(t + 1) * P, :], ytok[:, t, :]).then_inc(out_done, 16)
            act.wait_ge(fin_s, 5)
            act.dma_start(y_sample.rearrange("b s n -> (b s) n"), ys_tok).then_inc(out_done, 16)
            act.wait_ge(kv_out, 16 * 9 * NP_)
            act.wait_ge(out_done, OUT_ALL)

        @block.vector
        def _(dve):
            V = nc.vector
            ch = Chain(dve, dve_chain)

            def split_lo(st, it, c):
                dve.wait_ge(hi_done, st.chunk(it, c) + 1)
                k = split_tiles(st, c)
                V.tensor_tensor(wl[c % 2][:, 0:k], wraw[:, c % 4, 0:k], wh[c % 2][:, 0:k].bitcast(F32),
                                ALU.subtract).then_inc(split_done, 1)

            def splits(st, it, c, last=False):
                if last and c >= st.per_body - 2:
                    return
                for di, cc in ahead(st, c):
                    split_lo(st, it + di, cc)

            def gained(norm, m, n, last=False):
                hm = hh[:, bass.ds(m, 1)].rearrange("p o h n -> p (o h) n").bitcast(F32)
                xm = x[:, bass.ds(m, 1)].rearrange("p o h n -> p (o h) n")
                dve.wait_ge(h_ready, n + 1)
                V.scalar_tensor_tensor(out=hl[:, bass.ds(m, 1)].rearrange("p o h n -> p (o h) n"), in0=xm,
                                       scalar=params[:, bass.ds(m + GAIN[norm], 1)], in1=hm,
                                       op0=ALU.mult, op1=ALU.subtract).then_inc(hl_ready, 1)
                dve.wait_ge(sq_ready, n + 1)
                dve.wait_ge(ssq_ready, n + 1)
                V.tensor_tensor(ssq[:], ssq[:], sq, ALU.add).then_inc(ssq_ready, 1)

            def rms(norm):
                dve.wait_ge(ms_ready, 2 * norm + 1)
                V.tensor_scalar(r[:], N[:, :, 0:HALF], EPS, None, ALU.add).then_inc(ms_ready, 1)
                ch.after(V.memset(ssq[:], 0.0))
                dve.wait_ge(r_ready, norm + 1)

            def residual(st, it, c, par, m, n):
                xm = x[:, bass.ds(m, 1)].rearrange("p o h n -> p (o h) n")
                dve.wait_ge(chunk_used, st.chunk(it, c) + 1)
                V.tensor_tensor(xm, acc[:, par, :, 0:HALF], xm, ALU.add).then_inc(x_ready, 1)
                dve.wait_ge(x_ready, n + 1)
                dve.sem_inc(acc_free, 1)

            def taps(v, f, w1, w2):
                dve.wait_ge(c0_ready, v + 1)
                ch.after(V.scalar_tensor_tensor(out=cv[:], in0=u[:, 1:1 + CO], scalar=params[:, bass.ds(f + w1, 1)],
                                                in1=cv[:], op0=ALU.mult, op1=ALU.add))
                V.scalar_tensor_tensor(out=cv[:], in0=u[:, 2:2 + CO], scalar=params[:, bass.ds(f + w2, 1)],
                                       in1=cv[:], op0=ALU.mult, op1=ALU.add).then_inc(conv_done, 1)

            def y_lo(n, slot):
                dve.wait_ge(yh_ready, n + 1)
                V.tensor_tensor(yl_r[:, bass.ds(slot, 1)].rearrange("p o h n -> p (o h) n"), y32[:],
                                yh[:, bass.ds(slot, 1)].rearrange("p o h n -> p (o h) n"),
                                ALU.subtract).then_inc(yl_ready, 1)
                dve.wait_ge(yl_ready, n + 1)

            V.memset(small[:, 0:1], 0.0).then_inc(split_done, 4)
            V.memset(small[:, 7:8], EPS).then_inc(conv_done, 1)
            V.memset(u[:, 0:2], 0.0).then_inc(rows_kept, 1)
            V.memset(rb[NB:NB + 1, :], 1.0).then_inc(gain_ready, 1)
            V.memset(ssq[:], 0.0).then_inc(ssq_ready, 1)
            dve.wait_ge(setup_t, 1)
            V.tensor_copy(params[:], M[:, 0, 0:NPC])
            V.tensor_copy(hist_sc[:].rearrange("p x f -> p (x f)"), M[:, 1, 0:P])
            V.tensor_copy(hist_ffn[:].rearrange("p l x f -> p l (x f)"), acc[:, 1, :, 0:16 * FK]) \
                .then_inc(params_ready, 1)
            dve.wait_ge(params_ready, 1)
            V.memset(small[:, 0:1], 0.0).then_inc(acc_free, 2)
            dve.wait_ge(gains_in, 64)
            V.tensor_scalar(gq[:, 0:1], gq[:, 0:1], SCALE, None, ALU.mult).then_inc(gain_ready, 1)
            for c in range(2):
                split_lo(S_IN, 0, c)
            for m in range(DK):
                dve.wait_ge(xt_ready, m + 1)
                V.tensor_copy(x[:, m, :, 0:HP], M[:, m % 2, :].rearrange("p (h n) -> p h n", h=2))
                V.tensor_copy(x[:, m, :, HP:HALF], N[:, 0, m * NS:(m + 1) * NS].rearrange("p (h n) -> p h n", h=2)) \
                    .then_inc(x_ready, 1)
                gained(0, m, m)
                if m == 2:
                    dve.wait_ge(vec_mm, 1)
                    V.tensor_copy(vec_sb_t[:, 0:1024], acc[0:H, 1].rearrange("p h n -> p (h n)"))
                    V.tensor_copy(vec_sb_t[:, 1024:1536], acc[0:H, 0, 0, :]).then_inc(vec_sb, 1)
            rms(0)
            ch.end()

            bb, cc_, xx = t1, y32, sv[:, 0:2 * HALF].rearrange("p (h n) -> p h n", h=2)
            with dve.Fori(0, 2) as it:
                ch.begin(it, 12)
                for j in range(4):
                    v = it * 4 + j
                    for c, dst in enumerate((bb[:], cc_[:], xx)):
                        k = 3 * j + c
                        dve.wait_ge(chunk_used, S_IN.chunk(it, k) + 1)
                        V.tensor_tensor(dst, acc[:, k % 2, :, 0:HALF], r[:], ALU.mult).then_inc(acc_free, 1)
                        splits(S_IN, it, k)
                    dve.wait_ge(acc_free, S_IN.tile(it, 3 * j + 2) + 3)
                    dve.wait_ge(rows_kept, v + 1)
                    V.tensor_tensor(u_prompt, prompt(cc_), prompt(xx), ALU.mult)
                    V.tensor_tensor(u_new, sample(cc_), sample(xx), ALU.mult).then_inc(u_ready, 1)
                    dve.wait_ge(u_ready, v + 1)
                    taps(v, v, PC_SCW + DK, PC_SCW + 2 * DK)
                    dve.wait_ge(conv_done, v + 2)
                    ch.after(V.tensor_tensor(prompt(y32), prompt(bb), conv_prompt(cv), ALU.mult))
                    ch.after(V.tensor_tensor(sample(y32), sample(bb), conv_rows(cv), ALU.mult))
                    dve.sem_inc(y_ready, 1)
                    y_lo(v, v)
            ch.end(2)

            def rows_flush(n):
                dve.wait_ge(rows_t, n + 1)
                if n == 0:
                    V.tensor_copy(newh_tok[:, 0:P], N[:, 1, 0:P])
                    V.tensor_copy(newh_tok[0:16, P:2 * P], N[0:16, 1, P:2 * P]).then_inc(rows_tok, 1)
                else:
                    dve.wait_ge(out_done, 16 * (2 if n == 1 else 7 + NG))
                    nt = 18 * FK // 4
                    V.tensor_copy(newh_tok[0:nt, :], N[0:nt, 1, :]).then_inc(rows_tok, 1)

            rows_flush(0)

            with dve.Fori(0, 2) as it:
                for c in range(4):
                    m = it * 4 + c
                    residual(S_OUT, it, c, c % 2, m, m + DK)
                    splits(S_OUT, it, c)
                    gained(1, m, m + DK)
            ch.begin()
            rms(1)
            ch.end()

            def ffn(layer, gu, dn, v0, x0, next_norm, rows_n):
                pc = PC_L[layer]
                with dve.Fori(0, FK // 2) as it:
                    ch.begin(it, 6)
                    for i in range(2):
                        f = it * 2 + i
                        dve.wait_ge(chunk_used, gu.chunk(it, 2 * i) + 1)
                        dve.wait_ge(rows_kept, f + (v0 + 1))
                        V.tensor_tensor(u_prompt, acc[:, 0, :, 0:HP], prompt(r), ALU.mult)
                        V.tensor_tensor(u_new, acc[:, 0, :, HP:HALF], sample(r), ALU.mult).then_inc(u_ready, 1)
                        dve.wait_ge(u_ready, f + (v0 + 1))
                        dve.sem_inc(acc_free, 1)
                        splits(gu, it, 2 * i)
                        taps(f + v0, f, pc + FK, pc + 2 * FK)
                        dve.wait_ge(silu_ready, f + (layer * FK + 1))
                        V.tensor_tensor(prompt(t1), conv_prompt(sv), prompt(r), ALU.mult)
                        ch.after(V.tensor_tensor(sample(t1), conv_rows(sv), sample(r), ALU.mult))
                        dve.wait_ge(chunk_used, gu.chunk(it, 2 * i + 1) + 1)
                        ch.after(V.tensor_tensor(y32[:], acc[:, 1, :, 0:HALF], t1[:], ALU.mult))
                        dve.sem_inc(acc_free, 1)
                        dve.sem_inc(y_ready, 1)
                        splits(gu, it, 2 * i + 1)
                        y_lo(f + v0 + YOFF[layer], f)
                ch.end(FK // 2)
                rows_flush(rows_n)

                def down(it, last):
                    for c in range(12):
                        if c % 3 < 2:
                            dve.wait_ge(chunk_used, dn.chunk(it, c) + 1)
                            splits(dn, it, c, last)
                        else:
                            m = it * 4 + c // 3
                            residual(dn, it, c, (c // 3) % 2, m, m + x0)
                            splits(dn, it, c, last)
                            if next_norm is not None:
                                gained(next_norm, m, m + x0)
                if next_norm is None:
                    down(0, False)
                    down(1, True)
                else:
                    with dve.Fori(0, 2) as it:
                        down(it, False)
                    ch.begin()
                    rms(next_norm)
                    ch.end()

            ffn(0, S_GU0, S_DN0, DK, 2 * DK, 2, 1)

            def unit_pt(n, pt=PT):
                dve.wait_ge(pt_ready, n + 1)
                V.tensor_copy(pt[0], N[:, 0, :]).then_inc(pt_dve, 1)

            def unit_o(n, h2, cls, bank=M[:, 1, 2 * P:3 * P]):
                dve.wait_ge(o_ready, n + 1)
                s = slice(h2 * DH, h2 * DH + DH)
                dst = o32[s].rearrange("p h n -> p (h n)")[:, 0:SEQ].rearrange("p (i c) -> p i c", c=NCLS)[:, :, cls]
                V.tensor_copy(dst, bank[s, 0:P]).then_inc(o_kept, 1)

            def unit_softmax(n, h2, cls, between=None):
                dve.wait_ge(s_ready, n + 1)
                dve.sem_inc(softmax_steps, 1)
                b0 = NCLS - 1 - cls
                ch.after(V.tensor_tensor_reduce(out=lg[:, 0:512], in0=M[:, 0, :], in1=tb[:, h2, b0:b0 + SEQ],
                                                scale=-1.0, scalar=BIG, op0=ALU.add, op1=ALU.min,
                                                accum_out=small[:, 0:1]))
                dve.sem_inc(softmax_steps, 1)
                V.tensor_tensor_reduce(out=lg[:, 512:768], in0=M[:, 1, 0:256], in1=tb[:, h2, T0W:TBW],
                                       scale=-1.0, scalar=small[:, 0:1], op0=ALU.add, op1=ALU.min,
                                       accum_out=small[:, 1:2]).then_inc(neg_ready, 1)
                if between:
                    between()
                dve.wait_ge(e_ready, n + 1)
                ch.after(V.reciprocal(small[:, 3:4], small[:, 2:3]))
                V.tensor_scalar(pr[:], pr[:], small[:, 3:4], None, ALU.mult).then_inc(p_ready, 1)

            def tile_out(pair, c, i):
                g = c // 3
                dve.wait_ge(chunk_used, S_QKV.chunk(pair, c) + 1)
                a = acc[:, c % 2]
                if c % 3 < 2 or g == 0:
                    t = qk_t[:, i] if c % 3 < 2 else v_t[:, 0]
                    V.tensor_tensor(t[:, 0:SEQ].rearrange("p (h n) -> p h n", h=2), a[:, :, 0:HP], prompt(r),
                                    ALU.mult)
                else:
                    t = v_t[:, g]
                    o = t[:, 0:SEQ].rearrange("p (c h n) -> p h n c", c=NCLS, h=2)
                    V.tensor_tensor(o, a[:, :, 0:HP].rearrange("p h (n c) -> p h n c", c=NCLS),
                                    prompt(r).rearrange("p h (n c) -> p h n c", c=NCLS), ALU.mult)
                ch.after(V.tensor_tensor(t[:, SEQ:TT].rearrange("p (h n) -> p h n", h=2), a[:, :, HP:HALF],
                                         sample(r), ALU.mult))
                dve.sem_inc(acc_free, 1)
                if c % 3 < 2:
                    dve.sem_inc(qk_ready, 1)

            def project(pair, attend):
                i = 0
                for c in range(9):
                    n = (pair - 1) * 8
                    if attend and c >= 1:
                        unit_pt(n + c - 1)
                        unit_o(n + c - 1, *UNITS[c - 1])
                    if attend and c < 8:
                        unit_softmax(n + c, *UNITS[c])
                    if c == 8:
                        for k in range(5):
                            normalise(pair, k)
                    tile_out(pair, c, i)
                    if c % 3 < 2:
                        i += 1
                    if c < 8:
                        splits(S_QKV, pair, c)
                if attend:
                    pair_y(pair - 1)

            def pair_y(pair):
                dve.wait_ge(yh_ready, pair + (DK + FK + 1))
                dst = yl_r[:, bass.ds(pair, 1), :, 0:HP].rearrange("p o h n -> p (o h) n")
                src = yh[:, bass.ds(pair, 1), :, 0:HP].rearrange("p o h n -> p (o h) n")
                V.tensor_tensor(dst, o32[:].rearrange("p h n -> p (h n)")[:, 0:SEQ]
                                .rearrange("p (h n) -> p h n", h=2), src, ALU.subtract).then_inc(yl_ready, 1)

            def normalise(pair, i):
                g, isk = i // 2, i % 2
                dve.wait_ge(inv_ready, pair * 6 + (i + 1))
                o = qka[:, i, 0:SEQ]
                a, b = qk_t[:, i, 0:SEQ], inv[:, i, 0:SEQ]
                if not (g == 0 and isk):
                    o = o.rearrange("p (c n) -> p n c", c=NCLS)
                    a = a.rearrange("p (n c) -> p n c", c=NCLS)
                    b = b.rearrange("p (n c) -> p n c", c=NCLS)
                V.scalar_tensor_tensor(out=o, in0=a, scalar=gq[:, isk:isk + 1], in1=b, op0=ALU.mult, op1=ALU.mult)
                V.scalar_tensor_tensor(out=qka[:, i, SEQ:TT], in0=qk_t[:, i, SEQ:TT],
                                       scalar=gq[:, isk:isk + 1], in1=inv[:, i, SEQ:TT], op0=ALU.mult,
                                       op1=ALU.mult).then_inc(norm_ready, 1)

            def finish(pair):
                normalise(pair, 5)
                split_lo(S_QKV, pair + 1, 0)
                for i in range(3):
                    dve.wait_ge(kvt_ready, pair * 7 + 2 * i + 1)
                    V.tensor_copy(kv_tok[:, i, :, 0, :],
                                  (M, N, M)[i][:, 0, :].rearrange("p (t d) -> p t d", t=4)).then_inc(kvt_dve, 1)
                dve.wait_ge(kvt_ready, pair * 7 + 7)
                rows = acc[0:NS, 1].rearrange("p h (t d) -> p (h t) d", d=P)
                V.tensor_copy(q_s[0:NS, 0:2, bass.ds(pair * P, P)], rows[:, 6:8, :])
                V.tensor_copy(q_s[0:NS, 2, bass.ds(pair * P, P)], N[0:NS, 0, 0:P])
                V.tensor_copy(kv_s[:, :, :, bass.ds(pair * P, P)].rearrange("p g k d -> p (g k) d"), rows[:, 0:6, :]) \
                    .then_inc(kvt_dve, 1)
                split_lo(S_QKV, pair + 1, 1)

            dve.wait_ge(gain_ready, 2)
            ch.begin()
            project(0, False)
            ch.end()
            finish(0)
            with dve.Fori(1, NP_) as pair:
                ch.begin(pair - 1, 9 + 16)
                project(pair, True)
                dve.wait_ge(kv_out, pair * (16 * 9))
                finish(pair)
            ch.end(NP_ - 1)
            ch.begin()
            dve.wait_ge(rb_in, 32)
            for b in range(NS):
                last = V.tensor_copy(rbs[0:NB, :, b, :], rb[0:NB, :].rearrange("p (g h) -> p g h", g=NG))
            last.then_inc(samp_rb, 1)

            def key_products(b):
                dve.wait_ge(samp_in[b % 2], 16 * 8 * (b // 2 + 1))
                V.tensor_tensor(sprod[:, 0:2], skey[b % 2][:, 0:2], sq_b[b % 2][:, 0:2], ALU.mult)
                V.tensor_tensor(sprod[0:SK[2], 2], skey[b % 2][0:SK[2], 2], sq_b[b % 2][0:SK[2], 2],
                                ALU.mult).then_inc(samp_prod, 1)

            def key_sums(b):
                dve.wait_ge(samp_prod, b + 1)
                V.tensor_reduce(out=lt[:, 0:2, b * H:(b + 1) * H],
                                in_=sprod[:, 0:2].rearrange("p g (h d) -> p g h d", h=H), axis=AX_X, op=ALU.add)
                V.tensor_reduce(out=lt[0:SK[2], 2, b * H:(b + 1) * H],
                                in_=sprod[0:SK[2], 2].rearrange("p (h d) -> p h d", h=H), axis=AX_X,
                                op=ALU.add).then_inc(samp_lt, 1)
                dve.wait_ge(samp_lt, b + 1)

            def between(n):
                key_products(n - 1)
                unit_o((NP_ - 1) * 8 + n - 1, *UNITS[n - 1], acc[:, (n - 1) % 2, 0])

            for n in range(8):
                if n:
                    unit_pt((NP_ - 1) * 8 + n - 1, PT_LAST)
                unit_softmax((NP_ - 1) * 8 + n, *UNITS[n], between=(lambda n=n: between(n)) if n else None)
                if n:
                    key_sums(n - 1)
            key_products(NS - 1)
            unit_pt(NP_ * 8 - 1, PT_LAST)
            key_sums(NS - 1)
            ch.after(V.memset(pts, 0.0))
            unit_o(NP_ * 8 - 1, *UNITS[7], acc[:, 1, 0])
            pair_y(NP_ - 1)

            dve.wait_ge(samp_l, 1)
            ch.after(V.tensor_scalar(sl[0:64], M[0:64, 0, 0:NSC], -1.0, None, ALU.mult))
            V.tensor_reduce(out=small[0:64, 4:5], in_=sl[0:64], axis=AX_X, op=ALU.min).then_inc(samp_m, 1)
            dve.wait_ge(samp_e, 1)
            ch.after(V.reciprocal(small[0:64, 5:6], small[0:64, 5:6]))
            ch.after(V.tensor_scalar(se[0:64], se[0:64], small[0:64, 5:6], None, ALU.mult))
            dve.sem_inc(samp_p, 1)
            dve.wait_ge(samp_pt, 1)
            V.tensor_copy(pts[:, 0:2].rearrange("p g (b c) -> p g b c", b=NS)[:, :, :, 0:H],
                          M[:, 1, 0:2 * W].rearrange("p (g b h) -> p g b h", g=2, b=NS))
            V.tensor_copy(pts[0:SK[2], 2].rearrange("p (b c) -> p b c", b=NS)[:, :, 0:H],
                          M[0:SK[2], 1, 2 * W:3 * W].rearrange("p (b h) -> p b h", b=NS)).then_inc(samp_pts, 1)
            dve.wait_ge(samp_v, 1)
            V.tensor_copy(o_rows, acc[0:W, 0, 0, :]).then_inc(samp_rows_o, 1)
            dve.wait_ge(samp_heads, 1)
            V.tensor_copy(os_, N[:, 0, 0:NP_ * NS].rearrange("p (q b) -> p q b", q=NP_)).then_inc(samp_o, 1)
            dve.wait_ge(yh_ready, DK + FK + NP_ + 1)
            V.tensor_tensor(yl_r[:, 0:NP_, :, HP:HALF], os_.rearrange("p q (h n) -> p q h n", h=2),
                            yh[:, 0:NP_, :, HP:HALF], ALU.subtract).then_inc(yl_ready, 1)
            ch.end()

            with dve.Fori(0, 2) as it:
                for c in range(4):
                    m = it * 4 + c
                    residual(S_WO, it, c, c % 2, m, m + 3 * DK)
                    splits(S_WO, it, c)
                    gained(3, m, m + 3 * DK)
            ch.begin()
            rms(3)
            ch.end()
            ffn(1, S_GU1, S_DN1, DK + FK, 4 * DK, None, 2)

            for j in range(2):
                last = V.tensor_copy(xs_c[:, :, j * HS:(j + 1) * HS], x[:, :, j, HP:HALF])
            last.then_inc(fin_xs, 1)
            for t in range(4):
                dve.wait_ge(fin_t, t + 1)
                V.tensor_copy(ytok[:, t, :].rearrange("p (h n) -> p h n", h=2), (M, N)[t % 2][:]) \
                    .then_inc(fin_s, 1)
            dve.wait_ge(fin_t, 5)
            V.tensor_copy(ys_tok.rearrange("p (h n) -> p h n", h=2), M[0:NS]).then_inc(fin_s, 1)

        @block.tensor
        def _(pe):
            T = nc.tensor

            def transpose(out, in_):
                k = in_.shape[0]
                return T.transpose(out, in_, ident[0:k, 0:k])

            def products(st, it, c, par, nk, xh, xl, k0, first, last, inserts=None, free_d=2):
                g = st.chunk(it, c)
                pe.wait_ge(split_done, g + 5)
                for k in range(nk):
                    if inserts and k in inserts:
                        inserts[k]()
                    for n, (w, a) in enumerate(((wh, xh), (wh, xl), (wl, xh))):
                        for h2 in range(2):
                            ins = T.matmul(acc[:, par, h2, 0:HALF], w[c % 2][:, k, :], a[:, k0 + k, h2, :],
                                           start=(first and k == 0 and n == 0),
                                           stop=(last and k == nk - 1 and n == 2))
                ins.then_inc(chunk_used, 1)

            def free_acc(st, it, t, d=2):
                pe.wait_ge(acc_free, st.tile(it, t) + (3 - d))

            def mean_square(norm):
                pe.wait_ge(ssq_ready, (norm + 1) * DK + 1)
                for h2 in range(2):
                    ins = T.matmul(N[:, h2, 0:HALF], rms_ones[:], ssq[:, h2, :], start=True, stop=True)
                ins.then_inc(ms_ready, 1)

            def first_chunk(norm):
                def at(k):
                    pe.wait_ge(hl_ready, norm * DK + k + 1)
                    if k == DK - 1:
                        mean_square(norm)
                return {k: (lambda k=k: at(k)) for k in range(DK)}

            pe.wait_ge(pool_set, 6)
            pe.wait_ge(rows_in, 16 * 14)
            transpose(M[:, 0, 0:7 * DK], rows[0:7 * DK, 0, :])
            for i in range(2):
                transpose(M[:, 0, PC_L[i]:PC_L[i] + 4 * FK], rows[0:4 * FK, 1 + i, :])
                for j in range(3):
                    n = min(P, 16 * FK - j * P)
                    transpose(acc[:, 1, i, j * P:j * P + n], rows[0:n, 4 + 3 * i + j, :])
            transpose(M[:, 1, 0:P], rows[:, 3, :]).then_inc(setup_t, 1)
            pe.wait_ge(setup_in, 16 * 5)
            for m in range(DK):
                transpose(N[:, 0, m * NS:(m + 1) * NS], xs_in[:, m * P:(m + 1) * P])
            pe.wait_ge(params_ready, 1)
            for m in range(DK):
                if m >= 2:
                    pe.wait_ge(x_ready, m - 1)
                for t in range(4):
                    ins = transpose(M[:, m % 2, t * P:(t + 1) * P], xin[:, t, m * P:(m + 1) * P])
                ins.then_inc(xt_ready, 1)
                if m == 1:
                    pe.wait_ge(rb_in, 32)
                    pe.wait_ge(gain_ready, 1)
                    for g, lo, out in ((0, 0, acc[0:H, 1, 0, :]), (0, 512, acc[0:H, 1, 1, :]),
                                       (1, V0, acc[0:H, 0, 0, 0:256]), (2, V0 + 256, acc[0:H, 0, 0, 256:512])):
                        w = out.shape[-1]
                        ins = T.matmul(out, rb[:, g * H:(g + 1) * H], hotb[:, lo:lo + w], start=True, stop=True)
                    ins.then_inc(vec_mm, 1)
            pe.wait_ge(vec_sb, 1)

            for c in range(12):
                free_acc(S_IN, 0, c)
                products(S_IN, 0, c, c % 2, DK, hh, hl, 0, True, True, first_chunk(0) if c == 0 else None)
            with pe.Fori(1, 2) as it:
                for c in range(12):
                    free_acc(S_IN, it, c)
                    products(S_IN, it, c, c % 2, DK, hh, hl, 0, True, True)
            pe.wait_ge(rows_kept, DK + 1)
            transpose(N[:, 1, 0:P], newh[:, 0:P])
            transpose(N[0:16, 1, P:2 * P], newh[:, P:P + 16]).then_inc(rows_t, 1)
            pe.wait_ge(yl_ready, DK - 1)
            with pe.Fori(0, 2) as it:
                for c in range(4):
                    free_acc(S_OUT, it, c)
                    products(S_OUT, it, c, c % 2, DK, yh_r, yl_r, 0, True, True,
                             {DK - 1: lambda: pe.wait_ge(yl_ready, DK)} if c == 0 else None)
            pe.wait_ge(rows_tok, 1)

            def ffn(layer, gu, dn, y0, norm):
                for c in range(4):
                    free_acc(gu, 0, c)
                    products(gu, 0, c, c % 2, DK, hh, hl, 0, True, True, first_chunk(norm) if c == 0 else None)
                with pe.Fori(1, FK // 2) as it:
                    for c in range(4):
                        free_acc(gu, it, c)
                        products(gu, it, c, c % 2, DK, hh, hl, 0, True, True)
                pe.wait_ge(rows_kept, DK + (layer + 1) * FK + 1)
                nt = 18 * FK // 4
                for j in range(4):
                    ins = transpose(N[0:nt, 1, j * P:(j + 1) * P], newh[:, j * nt:(j + 1) * nt])
                ins.then_inc(rows_t, 1)
                with pe.Fori(0, 2) as it:
                    for c in range(12):
                        k0, k1 = DN_CUT[c % 3]
                        if c % 3 == 0:
                            free_acc(dn, it, c // 3)
                        waits = {}
                        if c < 3:
                            waits[0] = lambda n=min(k1, FK - 1): pe.wait_ge(yl_ready, y0 + n)
                        if c == 2:
                            waits[FK - 1 - k0] = lambda: pe.wait_ge(yl_ready, y0 + FK)
                        products(dn, it, c, (c // 3) % 2, k1 - k0, yh_r, yl_r, k0, c % 3 == 0, c % 3 == 2, waits)
                pe.wait_ge(rows_tok, layer + 2)

            ffn(0, S_GU0, S_DN0, DK, 1)

            def unit_logits(n, h2, cls, parts=(0, 1)):
                s = slice(h2 * DH, h2 * DH + DH)
                cq = slice(cls * P, (cls + 1) * P)
                if 0 in parts:
                    T.matmul(M[:, 0, :], qka[s, 0, cq], qka[s, 1, 0:SEQ], start=True, stop=True)
                if 1 not in parts:
                    return
                T.matmul(M[:, 1, 0:P], qka[s, 2, cq], qka[s, 3, cq], start=True, stop=True)
                T.matmul(M[:, 1, P:2 * P], qka[s, 4, cq], qka[s, 5, cq], start=True, stop=True).then_inc(s_ready, 1)

            def unit_transpose(n):
                pe.wait_ge(p_ready, n + 1)
                for j in range(6):
                    ins = transpose(N[:, j // 4, (j % 4) * P:(j % 4 + 1) * P], pr[:, j * P:(j + 1) * P])
                ins.then_inc(pt_ready, 1)

            def unit_values(n, h2, cls, bank=M[:, 1, 2 * P:3 * P], pt=PT):
                pe.wait_ge(pt_act, n + 1)
                pe.wait_ge(pt_dve, n + 1)
                s = slice(h2 * DH, h2 * DH + DH)
                T.matmul(bank[s, 0:P], kv_tok[:, 1, cls, 1, s], pt[1][:, 0:P], start=True, stop=False)
                T.matmul(bank[s, 0:P], kv_tok[:, 2, cls, 1, s], pt[1][:, P:2 * P], start=False, stop=False)
                for t in range(4):
                    lo, hi = 32 * t, min(32 * t + 64, P)
                    ins = T.matmul(bank[s, lo:hi], kv_tok[:, 0, t, 1, s], pt[0][:, t * P + lo:t * P + hi],
                                   start=False, stop=(t == 3))
                ins.then_inc(o_ready, 1)

            def head_sums(pair, i):
                pe.wait_ge(qsq_ready, pair * 6 + (i + 1))
                for h2 in range(2):
                    ins = T.matmul(N[:, h2, 0:HALF], head_ones[:], sq[:, h2, :], start=True, stop=True)
                ins.then_inc(qms_ready, 1)

            def project(pair, attend):
                i = [0]
                n0 = (pair - 1) * 8
                for c in range(9):
                    ins = first_chunk(2) if c == 0 and not attend else {}
                    if attend and c >= 1:
                        def tr(c=c):
                            if c > 1 and (c - 2) % 3 < 2:
                                pe.wait_ge(inv_ready, pair * 6 + i[0])
                            unit_transpose(n0 + c - 1)
                        ins[2] = tr

                        def vals(c=c):
                            if c > 1:
                                pe.wait_ge(o_kept, n0 + c - 1)
                            unit_values(n0 + c - 1, *UNITS[c - 1])
                        ins[4] = vals
                    if attend and c < 8:
                        def lgts(c=c):
                            if c == 0:
                                ready_to_attend(pair - 1)
                            else:
                                pe.wait_ge(neg_ready, n0 + c)
                            unit_logits(n0 + c, *UNITS[c])
                        ins[3 if c else 5] = lgts
                    if c >= 1 and (c - 1) % 3 < 2:
                        def hs():
                            if i[0] > 0:
                                pe.wait_ge(inv_ready, pair * 6 + i[0])
                            head_sums(pair, i[0])
                            i[0] += 1
                        ins[6] = hs
                    free_acc(S_QKV, pair, c, d=1 if c == 0 else 2)
                    if attend and c == 1:
                        pe.wait_ge(kvt_dve, pair * 4)
                    products(S_QKV, pair, c, c % 2, DK, hh, hl, 0, True, True, ins)

            def finish(pair):
                pe.wait_ge(acc_free, S_QKV.tile(pair, 8) + 3)
                pe.wait_ge(inv_ready, pair * 6 + 6)
                for g in range(NG):
                    pe.wait_ge(norm_ready, pair * 6 + (2 * g + 2))
                    for kv in range(2):
                        if g == 2:
                            pe.wait_ge(*((kvt_dve, pair * 4 + 1), (kvt_act, pair * 3 + 1))[kv])
                        src = qka[:, 2 * g + 1] if kv == 0 else v_t[:, g]
                        for t in range(4):
                            ins = transpose((M, N, M)[g][:, kv, t * P:(t + 1) * P], src[:, t * P:(t + 1) * P])
                        ins.then_inc(kvt_ready, 1)
                for j in range(8):
                    src = (qka[:, 2 * (j - 6)] if j >= 6 else v_t[:, j // 2] if j % 2 else qka[:, j + 1])
                    transpose(acc[0:NS, 1, j // 4, (j % 4) * P:(j % 4 + 1) * P], src[:, SEQ:TT])
                pe.wait_ge(kvt_dve, pair * 4 + 2)
                transpose(N[0:NS, 0, 0:P], qka[:, 4, SEQ:TT]).then_inc(kvt_ready, 1)

            def ready_to_attend(pair):
                pe.wait_ge(kvt_dve, pair * 4 + 4)
                pe.wait_ge(kvt_act, pair * 3 + 3)
                pe.wait_ge(tb_in, (pair + 1) * 16)

            project(0, False)
            finish(0)
            with pe.Fori(1, NP_) as pair:
                project(pair, True)
                pe.wait_ge(o_kept, pair * 8)
                finish(pair)
            n0 = (NP_ - 1) * 8
            ready_to_attend(NP_ - 1)
            unit_logits(n0, *UNITS[0])
            for n in range(8):
                if n < 7:
                    pe.wait_ge(neg_ready, n0 + n + 1)
                    unit_logits(n0 + n + 1, *UNITS[n + 1], parts=(0,))
                unit_transpose(n0 + n)
                if n < 7:
                    unit_logits(n0 + n + 1, *UNITS[n + 1], parts=(1,))
                if n >= 2:
                    pe.wait_ge(o_kept, n0 + n - 1)
                unit_values(n0 + n, *UNITS[n], acc[:, n % 2, 0], PT_LAST)

            pe.wait_ge(o_kept, n0 + 8)
            pe.wait_ge(samp_rb, 1)
            pe.wait_ge(samp_const, 16 * NG)
            pe.wait_ge(samp_lt, NS)
            for g in range(NG):
                cols = slice(SCOL[g], SCOL[g] + SK[g])
                with_bias = [g] if g < NG - 1 else list(range(NG))
                for n, gg in enumerate(with_bias):
                    T.matmul(M[0:64, 0, cols], rbs[0:NB, gg].rearrange("p b h -> p (b h)"), hots[gg][:, cols],
                             start=(n == 0), stop=False)
                ins = T.matmul(M[0:64, 0, cols], lt[0:SK[g], g, :], ident[0:SK[g], 0:SK[g]],
                               start=False, stop=True)
            ins.then_inc(samp_l, 1)
            pe.wait_ge(samp_p, 1)
            for g in range(NG):
                ins = transpose(M[0:SK[g], 1, g * 64:(g + 1) * 64], se[0:64, SCOL[g]:SCOL[g] + SK[g]])
            ins.then_inc(samp_pt, 1)
            pe.wait_ge(samp_pts, 1)
            pe.wait_ge(samp_vin, 16 * 4 * NS)
            for b in range(NS):
                for g in range(NG):
                    n = SK[g]
                    ins = T.matmul(acc[0:W, 0, 0, :], pts[0:n, g, W * b:W * (b + 1)], sval[b][0:n, g, :],
                                   start=(b == 0 and g == 0), stop=(b == NS - 1 and g == NG - 1))
            ins.then_inc(samp_v, 1)
            pe.wait_ge(samp_rows_o, 1)
            for h in range(H):
                q, s = h // 2, slice(h % 2 * DH, h % 2 * DH + DH)
                ins = T.matmul(N[s, 0, q * NS:(q + 1) * NS], o_rows[:, h * DH:(h + 1) * DH],
                               ident[0:W, 0:W].rearrange("p (b h) -> p h b", h=H)[:, h, :], start=True, stop=True)
            ins.then_inc(samp_heads, 1)

            pe.wait_ge(yl_ready, DK + FK + NP_ + 1)
            with pe.Fori(0, 2) as it:
                for c in range(4):
                    free_acc(S_WO, it, c, d=1 if c == 0 else 2)
                    products(S_WO, it, c, c % 2, NP_, yh_r, yl_r, 0, True, True)
            ffn(1, S_GU1, S_DN1, DK + FK + NP_ + 1, 3)

            pe.wait_ge(x_ready, 5 * DK)
            for t in range(4):
                if t >= 2:
                    pe.wait_ge(fin_s, t - 1)
                for k in range(DK):
                    ins = transpose((M, N)[t % 2][:, k // 4, (k % 4) * P:(k % 4 + 1) * P],
                                    x[:, k, t // 2, (t % 2) * P:(t % 2 + 1) * P])
                ins.then_inc(fin_t, 1)
            pe.wait_ge(fin_s, 3)
            pe.wait_ge(fin_xs, 1)
            for k in range(DK):
                ins = transpose(M[0:NS, k // 4, (k % 4) * P:(k % 4 + 1) * P], xs_c[:, k, :])
            ins.then_inc(fin_t, 1)


_INS = ['x_prompt', 'x_sample', 'state_sc_conv', 'cache_kv_d1', 'cache_kv_d4', 'cache_kv_d16', 'state_ffn_conv',
        'norm_mix', 'norm_ffn', 'sc_w_in', 'sc_conv_w', 'sc_w_out', 'attn_w_qkv', 'attn_q_norm', 'attn_k_norm',
        'attn_w_out', 'rel_bias', 'ffn_w_gate', 'ffn_w_up', 'ffn_conv_w', 'ffn_conv_b', 'ffn_w_down']
_OUTS = [(1, SEQ, D), (NS, 1, D), (1, 1, 2, D)] + [(1, 1, min(w, SEQ), 2, H, DH) for w, _ in GROUPS] + \
    [(2, 1, 2, FF), (1, NS, 2, D)] + [(1, NS, k, 2, H, DH) for k in KEEP] + [(2, NS, 2, FF)]


def kernel(**inputs):
    import numpy as _np
    import concourse.bacc as _bacc
    from concourse import mybir as _mybir
    from concourse.bass_utils import run_bass_kernel_spmd as _run

    nc = _bacc.Bacc("TRN2", target_bir_lowering=False, num_devices=1)
    given = [(name, inputs[name]) for name in _INS] + [("bias_onehot", bias_onehot()),
                                                       ("sample_onehot", sample_onehot())]
    arrays, args = {}, []
    for name, a in given:
        a = _np.ascontiguousarray(a)
        arrays[f"in_{name}_dram"] = a
        args.append(nc.dram_tensor(f"in_{name}_dram", a.shape, _mybir.dt.from_np(a.dtype), kind="ExternalInput").ap())
    for i, shape in enumerate(_OUTS):
        args.append(nc.dram_tensor(f"out_{i}_dram", shape, F32, kind="ExternalOutput").ap())
    build(nc, *args)
    got = _run(nc, [arrays], core_ids=[0]).results[0]
    return tuple(got[f"out_{i}_dram"] for i in range(len(_OUTS)))
```
